# Optimizing a Trainium2 kernel written in Bass

```python
import jax
import jax.numpy as jnp
from jax import lax
import numpy as np

D_MODEL = 1024
BATCH = 1
SEQ = 256
DEPTH = 2

N_MEM = 256
HEAD_DIM = 64
CONV_CH = D_MODEL // 2
CONV_GROUPS = CONV_CH // HEAD_DIM
CONV_K = 3
FOX_HEADS = (D_MODEL // 2) // HEAD_DIM
FOX_WIDTH = FOX_HEADS * HEAD_DIM
MIX_WIDTH = CONV_CH + FOX_WIDTH
IN_COLS = 3 * CONV_CH + 3 * FOX_WIDTH + FOX_HEADS
XA_HEADS = 4
XA_HEAD_DIM = 128
XA_WIDTH = XA_HEADS * XA_HEAD_DIM
D_FF = 2816
N_EXPERTS = 8
TOP_K = 2
Q_BLOCK = 128
EPS = 1e-6
N_DENSE = (DEPTH + 1) // 2
N_MOE = DEPTH // 2
SPLITS = (CONV_CH, 2 * CONV_CH, 3 * CONV_CH,
          3 * CONV_CH + FOX_WIDTH, 3 * CONV_CH + 2 * FOX_WIDTH, 3 * CONV_CH + 3 * FOX_WIDTH)

kernel_name = 'hybrid_conv_fox_memxattn_moe'

def rmsnorm(x, g):
    xf = x.astype(jnp.float32)
    y = xf * lax.rsqrt(jnp.mean(xf * xf, axis=-1, keepdims=True) + EPS)
    return (y * g.astype(jnp.float32)).astype(x.dtype)

def short_gated_conv(gate_b, gate_c, v, w):
    S = v.shape[1]
    u = gate_c * v
    up = jnp.pad(u, ((0, 0), (CONV_K - 1, 0), (0, 0)))
    y = w[0] * up[:, 0:S]
    for j in range(1, CONV_K):
        y = y + w[j] * up[:, j:j + S]
    return gate_b * y

def forgetting_attention(q, k, v, log_f):
    B, S, H, Dh = q.shape
    c = jnp.transpose(jnp.cumsum(log_f, axis=1), (0, 2, 1))
    n_blk = S // Q_BLOCK
    key_pos = jnp.arange(S)
    scale = Dh ** -0.5

    def block(i):
        start = i * Q_BLOCK
        qb = lax.dynamic_slice_in_dim(q, start, Q_BLOCK, axis=1)
        cb = lax.dynamic_slice_in_dim(c, start, Q_BLOCK, axis=2)
        s = jnp.einsum('bqhd,bkhd->bhqk', qb, k, preferred_element_type=jnp.float32) * scale
        s = s + cb[..., :, None] - c[..., None, :]
        q_pos = start + jnp.arange(Q_BLOCK)
        s = jnp.where(key_pos[None, :] <= q_pos[:, None], s, -jnp.inf)
        p = jax.nn.softmax(s, axis=-1).astype(v.dtype)
        return jnp.einsum('bhqk,bkhd->bqhd', p, v)

    out = lax.map(block, jnp.arange(n_blk))
    return jnp.moveaxis(out, 0, 1).reshape(B, S, H, Dh)

def mem_cross_attention(h, m, w_q, w_kv, g_q, g_k):
    B, S, _ = h.shape
    M = m.shape[1]
    q = rmsnorm((h @ w_q).reshape(B, S, XA_HEADS, XA_HEAD_DIM), g_q)
    kv = (m @ w_kv).reshape(B, M, 2, XA_HEADS, XA_HEAD_DIM)
    k = rmsnorm(kv[:, :, 0], g_k)
    v = kv[:, :, 1]
    s = jnp.einsum('bshd,bmhd->bhsm', q, k, preferred_element_type=jnp.float32) * (XA_HEAD_DIM ** -0.5)
    p = jax.nn.softmax(s, axis=-1).astype(v.dtype)
    return jnp.einsum('bhsm,bmhd->bshd', p, v).reshape(B, S, XA_WIDTH)

def swiglu(h, w_g, w_u, w_d):
    return (jax.nn.silu(h @ w_g) * (h @ w_u)) @ w_d

def moe_swiglu(h, w_r, b_r, w_g, w_u, w_d):
    B, S, D = h.shape
    t = h.reshape(B * S, D)
    logits = jnp.dot(t, w_r, preferred_element_type=jnp.float32) + b_r.astype(jnp.float32)
    top_v, top_i = lax.top_k(logits, TOP_K)
    top_w = jax.nn.softmax(top_v, axis=-1)
    gates = jnp.sum(jax.nn.one_hot(top_i, N_EXPERTS, dtype=jnp.float32) * top_w[..., None], axis=1)
    gates = gates.astype(h.dtype)
    out = jnp.zeros_like(t)
    for e in range(N_EXPERTS):
        out = out + gates[:, e:e + 1] * swiglu(t, w_g[e], w_u[e], w_d[e])
    return out.reshape(B, S, D)

def setup_inputs(seed: int = 0) -> dict:
    key = jax.random.key(seed)
    ks = iter(jax.random.split(key, 32))
    L = DEPTH

    def nrm(shape, fan_in):
        return jax.random.normal(next(ks), shape, jnp.float32) * (fan_in ** -0.5)

    def gain(shape):
        return 1.0 + 0.02 * jax.random.normal(next(ks), shape, jnp.float32)

    return {
        'x': jax.random.normal(next(ks), (BATCH, SEQ, D_MODEL), jnp.float32),
        'mem': jax.random.normal(next(ks), (BATCH, N_MEM, D_MODEL), jnp.float32),
        'g_mix': gain((L, D_MODEL)),
        'w_in': nrm((L, D_MODEL, IN_COLS), D_MODEL),
        'conv_w': nrm((L, CONV_K, CONV_CH), CONV_K),
        'b_f': jax.random.uniform(next(ks), (L, FOX_HEADS), jnp.float32, 1.0, 4.0),
        'g_q': gain((L, HEAD_DIM)),
        'g_k': gain((L, HEAD_DIM)),
        'g_conv_out': gain((L, CONV_CH)),
        'g_fox_out': gain((L, FOX_WIDTH)),
        'w_out': nrm((L, MIX_WIDTH, D_MODEL), MIX_WIDTH),
        'g_xa': gain((L, D_MODEL)),
        'g_mem': gain((L, D_MODEL)),
        'w_xq': nrm((L, D_MODEL, XA_WIDTH), D_MODEL),
        'w_xkv': nrm((L, D_MODEL, 2 * XA_WIDTH), D_MODEL),
        'g_xq': gain((L, XA_HEAD_DIM)),
        'g_xk': gain((L, XA_HEAD_DIM)),
        'w_xo': nrm((L, XA_WIDTH, D_MODEL), XA_WIDTH),
        'g_ffn': gain((L, D_MODEL)),
        'w_gate': nrm((N_DENSE, D_MODEL, D_FF), D_MODEL),
        'w_up': nrm((N_DENSE, D_MODEL, D_FF), D_MODEL),
        'w_down': nrm((N_DENSE, D_FF, D_MODEL), D_FF),
        'w_router': nrm((N_MOE, D_MODEL, N_EXPERTS), D_MODEL),
        'b_router': 0.01 * jax.random.normal(next(ks), (N_MOE, N_EXPERTS), jnp.float32),
        'we_gate': nrm((N_MOE, N_EXPERTS, D_MODEL, D_FF), D_MODEL),
        'we_up': nrm((N_MOE, N_EXPERTS, D_MODEL, D_FF), D_MODEL),
        'we_down': nrm((N_MOE, N_EXPERTS, D_FF, D_MODEL), D_FF),
    }

def reference(x, mem, g_mix, w_in, conv_w, b_f, g_q, g_k, g_conv_out, g_fox_out, w_out,
              g_xa, g_mem, w_xq, w_xkv, g_xq, g_xk, w_xo, g_ffn, w_gate, w_up, w_down,
              w_router, b_router, we_gate, we_up, we_down):
    B, S, _ = x.shape
    for l in range(DEPTH):
        h = rmsnorm(x, g_mix[l])
        z = h @ w_in[l]
        c_b, c_c, c_v, q, k, v, f_logit = jnp.split(z, SPLITS, axis=-1)
        y_conv = short_gated_conv(c_b, c_c, c_v, conv_w[l])
        y_conv = rmsnorm(y_conv.reshape(B, S, CONV_GROUPS, HEAD_DIM),
                         g_conv_out[l].reshape(CONV_GROUPS, HEAD_DIM)).reshape(B, S, CONV_CH)
        q = rmsnorm(q.reshape(B, S, FOX_HEADS, HEAD_DIM), g_q[l])
        k = rmsnorm(k.reshape(B, S, FOX_HEADS, HEAD_DIM), g_k[l])
        v = v.reshape(B, S, FOX_HEADS, HEAD_DIM)
        log_f = jax.nn.log_sigmoid(f_logit.astype(jnp.float32) + b_f[l].astype(jnp.float32))
        y_fox = forgetting_attention(q, k, v, log_f)
        y_fox = rmsnorm(y_fox, g_fox_out[l].reshape(FOX_HEADS, HEAD_DIM)).reshape(B, S, FOX_WIDTH)
        x = x + jnp.concatenate([y_conv, y_fox], axis=-1) @ w_out[l]
        hx = rmsnorm(x, g_xa[l])
        m = rmsnorm(mem, g_mem[l])
        x = x + mem_cross_attention(hx, m, w_xq[l], w_xkv[l], g_xq[l], g_xk[l]) @ w_xo[l]
        hf = rmsnorm(x, g_ffn[l])
        i = l // 2
        if l % 2 == 0:
            x = x + swiglu(hf, w_gate[i], w_up[i], w_down[i])
        else:
            x = x + moe_swiglu(hf, w_router[i], b_router[i], we_gate[i], we_up[i], we_down[i])
    return x


_drawn_inputs = setup_inputs


def setup_inputs(seed=0):
    import zlib

    import numpy as np

    out = dict(_drawn_inputs(seed))
    spreads = {}
    factors = {'g_conv_out': 2.751,
     'g_xa': 6.287,
     'g_mem': 8.0,
     'g_xq': 8.0,
     'g_xk': 4.613,
     'b_router': 26.728,
     'g_ffn': 5.292}
    for name, (base, spread) in spreads.items():
        noise = np.random.default_rng([zlib.crc32(name.encode()), seed]).standard_normal(out[name].shape)
        drawn = base * np.exp(spread * noise) if base else spread * noise
        out[name] = jnp.asarray(drawn.astype(out[name].dtype))
    for name, factor in factors.items():
        out[name] = (out[name] * factor).astype(out[name].dtype)
    return out
```

```python
from contextlib import ExitStack

import numpy as np

import concourse.bass as bass
from concourse import mybir

P = 128
F32 = mybir.dt.float32
I32 = mybir.dt.int32
U32 = mybir.dt.uint32
ALU = mybir.AluOpType
ACT = mybir.ActivationFunctionType
AX_X = mybir.AxisListType.X

EPS = 1e-6
HD = 64
XHD = 128
MASKED = -3.0e38
BANK = 512
NBANK = 8
NSLOT = 8
SLOT = 3072
ZCOLS = SLOT // 8
PASS_CAP = 128


def bcast_last(ap, n):
    return ap.unsqueeze(len(ap.shape)).to_broadcast([*ap.shape, n])


class PsumPlan:

    def __init__(self):
        self.at, self.uses, self.turn = {}, [0] * NBANK, 0

    def add(self, name):
        b = self.turn % NBANK
        self.turn += 1
        self.at[name] = (b, self.uses[b])
        self.uses[b] += 1


def layer_results(layer):
    names = [f"xT{i}" for i in range(4)] + ["f"]
    if layer == 0:
        names += [f"mT{i}" for i in range(4)]
    names += [f"qk{i}" for i in range(4)] + ["v0", "v1", "ssqk"]
    names += [f"conv{i}" for i in range(6)] + [f"bq{i}" for i in range(4)]
    names += [f"s{h}" for h in range(8)]
    names += ["mk0", "mk1", "mv0", "mv1", "ssc", "ssmk", "bc0", "bc1", "bmk0", "bmk1"]
    names += [f"pt{h}" for h in range(8)] + ["o0", "o1", "oT0", "oT1"] + [f"wo{i}" for i in range(4)]
    names += [f"yT{i}" for i in range(4)] + ["xq0", "xq1", "ssxq", "bxq0", "bxq1"]
    names += [f"xs{h}" for h in range(4)] + [f"xpt{h}" for h in range(4)] + ["xo0", "xo1"]
    names += [f"xw{i}" for i in range(4)] + [f"zT{i}" for i in range(4)]
    return names


def build(nc, x, mem, g_mix, w_in, conv_w, b_f, g_q, g_k, g_conv_out, g_fox_out, w_out,
          g_xa, g_mem, w_xq, w_xkv, g_xq, g_xk, w_xo, g_ffn, w_gate, w_up, w_down,
          w_router, b_router, we_gate, we_up, we_down, out):
    L, D, ICOLS = w_in.shape
    _, S, _ = x.shape
    DFF = w_gate.shape[2]
    NE = we_gate.shape[1]
    KT = D // P
    TT = S // P
    CC = conv_w.shape[2]
    FH = b_f.shape[1]
    XH = w_xo.shape[1] // XHD
    FT = DFF // P
    FB = -(-DFF // BANK)
    DROWS = SLOT // D
    DSLOT = -(-FT // DROWS)
    assert (L, KT, TT, FH, XH, mem.shape[1]) == (2, 8, 2, 8, 4, S)

    plan = PsumPlan()
    plan.add((0, "vec"))
    for l in range(L):
        for n in layer_results(l):
            plan.add((l, n))
        if l == 0:
            for n in ([f"g0{i}" for i in range(FB)] + [f"g1{i}" for i in range(FB)]
                      + [f"u0{i}" for i in range(FB)] + [f"u1{i}" for i in range(FB)]
                      + [f"hT0{i}" for i in range(FB)] + ["d00", "d01"]
                      + [f"hT1{i}" for i in range(FB)] + ["d10", "d11"]):
                plan.add((l, n))
        else:
            for n in ["r", "rank0", "rank1", "ga0", "ga1"]:
                plan.add((l, n))
    loop_base, start_turn = list(plan.uses), plan.turn
    pass_names = ([f"g{i}" for i in range(FB)] + [f"u{i}" for i in range(FB)] + ["GT"]
                  + [f"hT{i}" for i in range(FB)] + ["d0", "d1", "ga0", "ga1"] + [f"sc{i}" for i in range(4)])
    in_pass = PsumPlan()
    in_pass.turn = start_turn
    for n in pass_names:
        in_pass.add(n)

    fills = []
    fill_at = {}

    def add_fill(name, src, shape):
        fill_at[name] = len(fills)
        fills.append((src, shape))

    def z_src(l, c0):
        return w_in[l][:, c0:c0 + ZCOLS].rearrange("(k p) c -> p k c", p=P)

    for l in range(L):
        for s in range(8):
            add_fill((l, "z", s), z_src(l, (3 * CC + ZCOLS * s) if s < 4 else ZCOLS * (s - 4)), (KT, ZCOLS))
        for s in range(4):
            add_fill((l, "xkv", s), w_xkv[l][:, 256 * s:256 * s + 256].rearrange("(k p) c -> p k c", p=P), (KT, 256))
        for s in range(4):
            add_fill((l, "wo", s), w_out[l][256 * s:256 * s + 256].rearrange("(k p) c -> p k c", p=P), (2, D))
        for s in range(2):
            add_fill((l, "xq", s), w_xq[l][:, 256 * s:256 * s + 256].rearrange("(k p) c -> p k c", p=P), (KT, 256))
        for s in range(2):
            add_fill((l, "xo", s), w_xo[l][256 * s:256 * s + 256].rearrange("(k p) c -> p k c", p=P), (2, D))
        if l == 0:
            for k in range(KT):
                add_fill((l, "g", k), w_gate[0][P * k:P * k + P].unsqueeze(1), (1, DFF))
            for k in range(KT):
                add_fill((l, "u", k), w_up[0][P * k:P * k + P].unsqueeze(1), (1, DFF))
            for s in range(DSLOT):
                k = min(DROWS, FT - DROWS * s)
                add_fill((l, "d", s), w_down[0][P * DROWS * s:P * (DROWS * s + k)].rearrange("(k p) c -> p k c", p=P), (k, D))
    NSTATIC = len(fills)
    frees = {}
    for l in range(L):
        for s, n in enumerate(["qk1", "qk2", "v1", "v1", "conv1", "conv2", "conv4", "conv5"]):
            frees[l, "z", s] = n
        for s, n in enumerate(["mk0", "mk1", "mv1", "mv1"]):
            frees[l, "xkv", s] = n
        frees.update({(l, "wo", 3): "wo3", (l, "xq", 0): "xq0", (l, "xq", 1): "xq1", (l, "xo", 1): "xw3"})
    frees.update({(0, "g", KT - 1): f"g1{FB - 1}", (0, "u", KT - 1): f"u1{FB - 1}", (0, "d", DSLOT - 1): "d11"})
    fill_names = list(fill_at)
    used_count, slots_used_total = {}, 0
    for name in fill_names:
        if name not in frees:
            slots_used_total += 1
            used_count[name] = slots_used_total
    PASS_FILLS = 2 * KT + DSLOT
    assert PASS_FILLS % NSLOT == 0 and NSTATIC % NSLOT == 0

    with ExitStack() as ctx:
        def sb(name, shape, dt=F32):
            return ctx.enter_context(nc.sbuf_tensor(name, shape, dt))

        def sem(name):
            return ctx.enter_context(nc.semaphore(name))

        ring = sb("ring", [P, NSLOT, SLOT])
        xres = sb("xres", [P, TT, D])
        xn = sb("xn", [P, TT, D])
        hT = sb("hT", [P, KT, S])
        memT = sb("memT", [P, KT, S])
        scratch = sb("scratch", [P, 13 * 1024])
        xk = sb("xk", [P, XH, S])
        xv = sb("xv", [P, 2, XH * XHD])
        psum = [ctx.enter_context(nc.psum_tensor(f"bank{b}", [P, BANK], F32)) for b in range(NBANK)]

        def part(at, *shape):
            n = int(np.prod(shape))
            ap = scratch[:, at:at + n]
            if len(shape) == 1:
                return ap
            names = "abc"[:len(shape)]
            return ap.rearrange(f"p ({' '.join(names)}) -> p {' '.join(names)}",
                                **{n_: s_ for n_, s_ in zip(names, shape)})

        zc = part(0, 12, S)
        zqk = part(3072, 8, S)
        sq = part(5120, 8, S)
        memraw = part(5120, TT, D)
        sc = part(5120, FH, 3 * P)
        osq = part(5120, TT * FH, HD)
        vtok = part(8192, 2, FH * HD)
        decay = part(9216, FH, 3 * P)
        pT = part(9216, FH, 3 * P)
        otok = part(12288, TT, FH * HD)
        ksq = part(12288, XH, S)
        yT = xn[:].rearrange("p t (k s) -> p (t k) s", s=S)
        xsc = part(5120, XH, 2, S)
        xpT = part(9216, XH, 2, S)
        hid = part(0, 2, DFF)
        hidT = part(2 * DFF, 2, FT, P)
        h1 = part(0, DFF)
        h1T = part(DFF, FT, P)
        xg = part(2 * DFF, KT, PASS_CAP)
        oneh = part(2 * DFF + 1024, TT, PASS_CAP)
        gated = part(2 * DFF + 1280, TT, PASS_CAP)
        gatedT = part(2 * DFF + 1536, S)
        yexp = part(2 * DFF + 1792, D)

        ident = sb("ident", [P, P])
        tri8 = sb("tri8", [P, S])
        after = sb("after", [P, 3 * P])
        mask = sb("mask", [P, 3 * P])
        selg = sb("selg", [P, 30])
        selh = sb("selh", [P, 7])
        spreadg = sb("spreadg", [16, 8 * P])
        spreadh = sb("spreadh", [4, 4 * P])
        ones1 = sb("ones1", [1, P])
        neghalf = sb("neghalf", [P, 1])
        place = sb("place", [P, PASS_CAP])
        eight = sb("eight", [P, NE])
        NV = 56
        vrows = sb("vrows", [2 * NV, P])
        vcols = sb("vcols", [P, 2 * NV])
        wf = sb("wf", [P, L, KT, FH])
        wr = sb("wr", [P, KT, NE])
        brow = sb("brow", [1, L * FH + NE])
        msq = sb("msq", [P, 8])
        mqk = sb("mqk", [16, S])
        mcv = sb("mcv", [8, S])
        mmk = sb("mmk", [4, S])
        mxq = mmk
        newton = sb("newton", [16, S])
        epscol = sb("epscol", [16, 1])
        mfox = sb("mfox", [P, TT * FH])
        fz = sb("fz", [P, 4, TT * FH])
        negmax = sb("negmax", [P, 2, FH])
        denom = sb("denom", [P, 2, FH])
        xnm = sb("xnm", [P, XH, 2])
        xden = sb("xden", [P, XH, 2])
        top = sb("top", [P, TT, 8])
        topi = sb("topi", [P, TT, 8], U32)
        topf = sb("topf", [P, TT, 8])
        logit = sb("logit", [P, TT, NE])
        gw = sb("gw", [P, TT, 4])
        hot = sb("hot", [P, TT, 3, NE])
        gates = sb("gates", [P, TT, 2 * NE + 1])
        pos = sb("pos", [P, TT, 2 * NE + 1])
        cnt = sb("cnt", [1, 4])
        npass = sb("npass", [1, 1], I32)

        vec, nrow = {}, 0
        for nm, k in (("mix", 8), ("xa", 8), ("mem", 8), ("ffn", 8), ("tap", 12), ("cv", 4), ("fox", 4),
                      ("xq", 1), ("xk", 1), ("q", 1), ("k", 1)):
            for l in range(L):
                vec[l, nm] = nrow
                nrow += k
        assert nrow == 2 * NV

        def col(l, nm, i=0, n=1):
            return vcols[:, vec[l, nm] + i:vec[l, nm] + i + n]

        psum_full = [sem(f"psum_full{b}") for b in range(NBANK)]
        psum_taken = [sem(f"psum_taken{b}") for b in range(NBANK)]
        slot_filled = [sem(f"slot_filled{s}") for s in range(NSLOT)]
        slots_used = sem("slots_used")
        x_loaded = sem("x_loaded")
        mem_loaded = sem("mem_loaded")
        params_loaded = sem("params_loaded")
        pool_step = sem("pool_step")
        dve_step = sem("dve_step")
        act_step = sem("act_step")
        consts_ready = sem("consts_ready")
        ident_ready = sem("ident_ready")
        meansq_ready = sem("meansq_ready")
        rstd_ready = sem("rstd_ready")
        guess_ready = sem("guess_ready")
        rows_ready = sem("rows_ready")
        xn_ready = sem("xn_ready")
        fabs_ready = sem("fabs_ready")
        fln_ready = sem("fln_ready")
        logf_ready = sem("logf_ready")
        decay_ready = sem("decay_ready")
        squares_ready = sem("squares_ready")
        qk_ready = sem("qk_ready")
        memg_ready = sem("memg_ready")
        negmax_ready = sem("negmax_ready")
        probs_ready = sem("probs_ready")
        conv_ready = sem("conv_ready")
        osum_ready = sem("osum_ready")
        onorm_ready = sem("onorm_ready")
        xmax_ready = sem("xmax_ready")
        xprobs_ready = sem("xprobs_ready")
        xpn_ready = sem("xpn_ready")
        topd_ready = sem("topd_ready")
        tope_ready = sem("tope_ready")
        sel_ready = sem("sel_ready")
        route_ready = sem("route_ready")
        oneh_ready = sem("oneh_ready")
        gated_ready = sem("gated_ready")
        stored = sem("stored")

        RSTDS = {}
        ROWS = {}
        SQUARES = {}
        for l in range(L):
            for n in ["mix"] + (["mem"] if l == 0 else []) + ["fox", "xa", "ffn"]:
                RSTDS[l, n] = len(RSTDS) + 1
            for n in ["qk0", "qk1", "qk2", "qk3", "mk", "cv", "fox", "xq"]:
                SQUARES[l, n] = len(SQUARES) + 1
            for n in ["qk", "cv", "mk", "xq"]:
                ROWS[l, n] = len(ROWS) + 1

        XN = {}
        for n in [(0, "mix"), (0, "mem"), (0, "xa"), (0, "ffn"), (1, "mix"), (1, "xa"), (1, "ffn")]:
            XN[n] = TT * (len(XN) + 1)
        NPARAMS = 18

        def bank(l, n):
            return psum[plan.at[l, n][0]]

        def full(l, n):
            b, use = plan.at[l, n]
            return psum_full[b], use + 1

        def taken(l, n):
            b, use = plan.at[l, n]
            return psum_taken[b], use + 1

        def take(l, n):
            return psum_taken[plan.at[l, n][0]]

        def lbank(n):
            return psum[in_pass.at[n][0]]

        def lcount(n, p):
            b, use = in_pass.at[n]
            return p * in_pass.uses[b] + (loop_base[b] + use)

        def lfull(n, p):
            return psum_full[in_pass.at[n][0]], lcount(n, p) + 1

        def ltaken(n, p):
            return psum_taken[in_pass.at[n][0]], lcount(n, p) + 1

        def ltake(n):
            return psum_taken[in_pass.at[n][0]]

        block = ctx.enter_context(nc.Block())

        @block.sync
        def _(sp):
            def slot_free(name):
                if name in frees:
                    sp.wait_ge(*full(name[0], frees[name]))
                else:
                    sp.wait_ge(slots_used, used_count[name])

            def slot_free_in_pass(j, p):
                if j < 0:
                    j, p = j + PASS_FILLS, p - 1
                ends = {KT - 1: f"g{FB - 1}", 2 * KT - 1: f"u{FB - 1}", PASS_FILLS - 1: "d1"}
                if j in ends:
                    sp.wait_ge(*lfull(ends[j], p))
                else:
                    before = sum(1 for k in ends if k < j)
                    sp.wait_ge(slots_used, p * (PASS_FILLS - 3) + (slots_used_total + j - before + 1))

            sp.dma_start(xres[:], x[0].rearrange("(t p) d -> p t d", p=P)).then_inc(x_loaded, 16)
            for n, (src, (k, c)) in enumerate(fills):
                if n >= NSLOT:
                    slot_free(fill_names[n - NSLOT])
                dst = ring[:, n % NSLOT, 0:k * c].rearrange("p (k c) -> p k c", k=k)
                sp.dma_start(dst, src).then_inc(slot_filled[n % NSLOT], 16)
                if n == 1:
                    sp.wait_ge(params_loaded, 16 * NPARAMS)
                    sp.dma_start(memraw, mem[0].rearrange("(t p) d -> p t d", p=P)).then_inc(mem_loaded, 16)

            wg_rows = we_gate[0].rearrange("e d f -> (e d) f")
            wu_rows = we_up[0].rearrange("e d f -> (e d) f")
            wd_rows = we_down[0].rearrange("e (k p) c -> p (e k) c", p=P)
            sp.wait_ge(route_ready, 1)
            rounds = sp.value_load(npass[0:1, 0:1], min_val=1, max_val=2)
            def load_expert(e, p, j):
                slot = (NSTATIC + j) % NSLOT
                if j < 2 * KT:
                    rows = wg_rows if j < KT else wu_rows
                    sp.dma_start(ring[:, slot, 0:DFF], rows[bass.ds(e * D + (j % KT) * P, P), :]
                                 ).then_inc(slot_filled[slot], 16)
                else:
                    k0 = (j - 2 * KT) * DROWS
                    k = min(DROWS, FT - k0)
                    dst = ring[:, slot, 0:k * D].rearrange("p (k c) -> p k c", k=k)
                    sp.dma_start(dst, wd_rows[:, bass.ds(e * FT + k0, k), :]).then_inc(slot_filled[slot], 16)

            for j in range(NSLOT):
                slot_free(fill_names[NSTATIC - NSLOT + j])
                load_expert(0, 0, j)
            sp.wait_ge(route_ready, 1)
            rounds = sp.value_load(npass[0:1, 0:1], min_val=1, max_val=2)
            with sp.Fori(0, rounds) as rnd:
                with sp.Fori(0, NE) as e:
                    p = rnd * NE + e
                    for j in range(NSLOT, PASS_FILLS):
                        slot_free_in_pass(j - NSLOT, p)
                        load_expert(e, p, j)
                    for j in range(NSLOT):
                        slot_free_in_pass(j + PASS_FILLS - NSLOT, p)
                        load_expert((e + 1) % NE, p, j)
            for i in range(4):
                sp.wait_ge(*ltaken(f"sc{i}", rounds * NE - 1))
            for s in range(NSLOT):
                sp.wait_ge(slot_filled[s], rounds * (16 * NE * (PASS_FILLS // NSLOT)) + 16 * (NSTATIC // NSLOT + 1))
            sp.dma_start(out[0].rearrange("(t p) d -> p t d", p=P), xres[:]).then_inc(stored, 16)
            sp.wait_ge(stored, 16)

        @block.gpsimd
        def _(pool):
            steps = [0]

            def then_wait(ins):
                steps[0] += 1
                ins.then_inc(pool_step, 1)
                pool.wait_ge(pool_step, steps[0])

            def select(ap, pattern, op, fill, base, mult):
                return nc.gpsimd.affine_select(out=ap, in_=ap, pattern=pattern, compare_op=op, fill=fill,
                                               base=base, channel_multiplier=mult)

            then_wait(nc.gpsimd.memset(ident[:], 0.0))
            select(ident[:], [[-1, P]], ALU.not_equal, 1.0, 0, 1).then_inc(ident_ready, 1)
            nc.gpsimd.memset(ones1[:], 1.0)
            nc.gpsimd.memset(neghalf[:], -0.5)
            nc.gpsimd.memset(epscol[:], EPS)
            nc.gpsimd.memset(tri8[:], 8.0)
            nc.gpsimd.memset(after[:], 1.0)
            nc.gpsimd.memset(mask[:], 0.0)
            nc.gpsimd.memset(selg[:], 0.0)
            nc.gpsimd.memset(selh[:], 0.0)
            nc.gpsimd.memset(spreadg[:], 1.0)
            then_wait(nc.gpsimd.memset(spreadh[:], 1.0))
            nc.gpsimd.memset(selh[:, 3:4], 1.0 / XHD)
            then_wait(nc.gpsimd.memset(selg[:, 14:16], 1.0 / HD))
            select(selg[:, 14:15], [[0, 1]], ALU.is_ge, 0.0, HD - 1, -1)
            select(selg[:, 15:16], [[0, 1]], ALU.is_ge, 0.0, -HD, 1)
            select(tri8[:], [[1, S]], ALU.is_ge, 0.0, 0, -1)
            for c in (0, 2 * P):
                select(after[:, c:c + P], [[-1, P]], ALU.is_gt, 0.0, 0, 1)
                select(mask[:, c:c + P], [[-1, P]], ALU.is_ge, MASKED, 0, 1)
            select(spreadg[:], [[1, 8 * P]], ALU.is_ge, 0.0, 0, -HD)
            then_wait(select(spreadh[:], [[1, 4 * P]], ALU.is_ge, 0.0, 0, -XHD))
            select(spreadg[:], [[-1, 8 * P]], ALU.is_ge, 0.0, HD - 1, HD)
            then_wait(select(spreadh[:], [[-1, 4 * P]], ALU.is_ge, 0.0, XHD - 1, XHD))
            nc.gpsimd.iota(place[:], [[1, PASS_CAP]], base=0, channel_multiplier=0,
                           allow_small_or_imprecise_dtypes=True)
            nc.gpsimd.iota(eight[:], [[1, NE]], base=0, channel_multiplier=0,
                           allow_small_or_imprecise_dtypes=True).then_inc(consts_ready, 1)

            def rstd(ap):
                then_wait(nc.gpsimd.tensor_scalar(ap, ap, EPS, None, ALU.add))
                rows, n = ap.shape
                nc.gpsimd.tensor_tensor(ap, ap, neghalf[0:rows, :].to_broadcast([rows, n]), ALU.pow).then_inc(rstd_ready, 1)

            norms = 0
            for l in range(L):
                norms += TT
                pool.wait_ge(meansq_ready, norms)
                rstd(msq[:, 0:2])
                if l == 0:
                    norms += TT
                    pool.wait_ge(meansq_ready, norms)
                    rstd(msq[:, 2:4])
                pool.wait_ge(logf_ready, l + 1)
                nc.gpsimd.tensor_tensor(
                    decay[:, :, 0:S], tri8[:].unsqueeze(1).to_broadcast([P, FH, S]),
                    bcast_last(fz[:, 3, 0:FH], S), ALU.mult)
                nc.gpsimd.tensor_tensor(
                    decay[:, :, S:3 * P], tri8[:, 0:P].unsqueeze(1).to_broadcast([P, FH, P]),
                    bcast_last(fz[:, 3, FH:2 * FH], P), ALU.mult).then_inc(decay_ready, 1)
                pool.wait_ge(*full(l, "conv5"))
                if l == 0:
                    pool.wait_ge(*taken(0, "vec"))
                    for i in range(4):
                        pool.wait_ge(*taken(0, f"mT{i}"))
                nc.gpsimd.tensor_tensor(hT[:], memT[:], bcast_last(col(l, "mem", 0, KT), S), ALU.mult
                                        ).then_inc(memg_ready, 1)
                pool.wait_ge(osum_ready, l + 1)
                rstd(mfox[:])
                norms += TT
                pool.wait_ge(meansq_ready, norms)
                rstd(msq[:, 0:2])
                norms += TT
                pool.wait_ge(meansq_ready, norms)
                rstd(msq[:, 0:2])

        @block.scalar
        def _(act):
            steps = [0]

            def then_wait(ins):
                steps[0] += 1
                ins.then_inc(act_step, 1)
                act.wait_ge(act_step, steps[0])

            for nm, src in (("mix", g_mix), ("xa", g_xa), ("mem", g_mem), ("ffn", g_ffn), ("cv", g_conv_out),
                            ("fox", g_fox_out), ("xq", g_xq), ("xk", g_xk)):
                r, k = vec[0, nm], L * src.shape[1] // P
                act.dma_start(vrows[r:r + k, :], src.rearrange("l (k p) -> (l k) p", p=P)).then_inc(params_loaded, 16)
            r = vec[0, "tap"]
            act.dma_start(vrows[r:r + 12 * L, :], conv_w.rearrange("l j (k p) -> (l j k) p", p=P)).then_inc(params_loaded, 16)
            for nm, src in (("q", g_q), ("k", g_k)):
                r = vec[0, nm]
                for half in range(2):
                    act.dma_start(vrows[r:r + L, half * HD:half * HD + HD], src).then_inc(params_loaded, 16)
            for l in range(L):
                act.dma_start(wf[:, l], w_in[l][:, ICOLS - FH:ICOLS].rearrange("(k p) c -> p k c", p=P)).then_inc(params_loaded, 16)
            act.dma_start(brow[0:1, 0:L * FH], b_f.rearrange("l h -> (l h)").unsqueeze(0)).then_inc(params_loaded, 16)
            act.dma_start(wr[:], w_router[0].rearrange("(k p) c -> p k c", p=P)).then_inc(params_loaded, 16)
            act.dma_start(brow[0:1, L * FH:L * FH + NE], b_router[0:1, :]).then_inc(params_loaded, 16)

            def square(l, n, dst, src, scale=1.0):
                nc.scalar.activation(dst, src, ACT.Square, scale=scale).then_inc(squares_ready, 1)

            def mean_squares(l, added):
                for t in range(TT):
                    for n in added[2 * t:2 * t + 2]:
                        if (l, n[:2]) == (0, "d0") or (l, n[:2]) == (0, "d1"):
                            continue
                        act.wait_ge(*taken(0 if n[0] == "d" else l, n))
                    nc.scalar.activation(xn[:, t, :], xres[:, t, :], ACT.Square, scale=D ** -0.5,
                                         accum_out=msq[:, t:t + 1]).then_inc(meansq_ready, 1)

            def guess_rows(l, n, result, dst):
                rows = dst.shape[0]
                act.wait_ge(*full(l, result))
                then_wait(nc.scalar.activation(dst, bank(l, result)[0:rows, 0:S], ACT.Ln, bias=epscol[0:rows, :]))
                nc.scalar.activation(dst, dst, ACT.Exp, scale=-0.5).then_inc(guess_ready, 1)

            def gained(l, names, gain):
                for i in (1, 3):
                    act.wait_ge(*full(l, f"{names}{i}"))
                    for k in range(2):
                        c = 2 * i + k
                        ins = nc.scalar.activation(hT[:, c, :], bank(l, f"{names}{i}")[:, k * S:k * S + S], ACT.Copy,
                                                   scale=col(l, gain, c))
                    ins.then_inc(take(l, f"{names}{i}"), 1)

            for l in range(L):
                if l == 0:
                    act.wait_ge(x_loaded, 16)
                mean_squares(l, ["d00", "d01", "d10", "d11"])
                if l == 0:
                    act.wait_ge(mem_loaded, 16)
                    for t in range(TT):
                        nc.scalar.activation(memT[:].rearrange("p k s -> p (k s)")[:, t * D:t * D + D], memraw[:, t, :],
                                             ACT.Square, scale=D ** -0.5,
                                             accum_out=msq[:, 2 + t:3 + t]).then_inc(meansq_ready, 1)
                    act.wait_ge(*taken(0, "vec"))
                gained(l, "xT", "mix")
                act.wait_ge(fabs_ready, l + 1)
                then_wait(nc.scalar.activation(fz[:, 2, :], fz[:, 1, :], ACT.Exp))
                nc.scalar.activation(fz[:, 2, :], fz[:, 2, :], ACT.Ln, bias=1.0).then_inc(fln_ready, 1)
                for i in range(4):
                    act.wait_ge(*taken(l, f"qk{i}"))
                    square(l, f"qk{i}", sq[:, 2 * i:2 * i + 2, :], zqk[:, 2 * i:2 * i + 2, :])
                for i in range(2):
                    act.wait_ge(*full(l, f"v{i}"))
                    nc.scalar.activation(vtok[:, i, :], bank(l, f"v{i}")[:], ACT.Copy).then_inc(take(l, f"v{i}"), 1)
                guess_rows(l, "qk", "ssqk", mqk[:])
                for i in range(4):
                    act.wait_ge(*full(l, f"conv{i}"))
                    nc.scalar.activation(zc[:, 2 * i:2 * i + 2, :].rearrange("p a s -> p (a s)"), bank(l, f"conv{i}")[:],
                                         ACT.Copy).then_inc(take(l, f"conv{i}"), 1)
                for h in range(FH):
                    act.wait_ge(negmax_ready, 4 * l + 2 * (h // 4 + 1))
                    for q, (a, b) in enumerate(((0, P), (P, 3 * P))):
                        nc.scalar.activation(sc[:, h, a:b], sc[:, h, a:b], ACT.Exp, bias=negmax[:, q, h:h + 1],
                                             accum_out=denom[:, q, h:h + 1]).then_inc(probs_ready, 1)
                for i in range(2):
                    act.wait_ge(*full(l, f"mk{i}"))
                    nc.scalar.activation(xk[:, 2 * i:2 * i + 2, :].rearrange("p a s -> p (a s)"), bank(l, f"mk{i}")[:],
                                         ACT.Copy).then_inc(take(l, f"mk{i}"), 1)
                for i in range(2):
                    act.wait_ge(*taken(l, f"mk{i}"))
                square(l, "mk", ksq, xk[:])
                for i in range(2):
                    act.wait_ge(*full(l, f"mv{i}"))
                    nc.scalar.activation(xv[:, i, :], bank(l, f"mv{i}")[:], ACT.Copy).then_inc(take(l, f"mv{i}"), 1)
                act.wait_ge(conv_ready, l + 1)
                square(l, "cv", zc[:, 4:8, :], zc[:, 0:4, :])
                guess_rows(l, "cv", "ssc", mcv[:])
                guess_rows(l, "mk", "ssmk", mmk[:])
                for h in range(1, FH, 2):
                    act.wait_ge(*full(l, f"pt{h}"))
                    nc.scalar.activation(pT[:, h, :], bank(l, f"pt{h}")[:, 0:3 * P], ACT.Copy).then_inc(take(l, f"pt{h}"), 1)
                for i in range(2):
                    act.wait_ge(*taken(l, f"o{i}"))
                square(l, "fox", osq.rearrange("p a b -> p (a b)"), otok.rearrange("p a b -> p (a b)"), scale=HD ** -0.5)

                mean_squares(l, [f"wo{i}" for i in range(4)])
                gained(l, "yT", "xa")
                for i in range(2):
                    act.wait_ge(*taken(l, f"xq{i}"))
                square(l, "xq", sq[:, 0:4, :], zqk[:, 0:4, :])
                guess_rows(l, "xq", "ssxq", mxq[:])
                for h in range(XH):
                    act.wait_ge(xmax_ready, XH * l + h + 1)
                    for q in range(2):
                        ins = nc.scalar.activation(xsc[:, h, q, :], bank(l, f"xs{h}")[:, q * S:q * S + S], ACT.Exp,
                                                   bias=xnm[:, h, q:q + 1], scale=XHD ** -0.5,
                                                   accum_out=xden[:, h, q:q + 1])
                        if q == 0:
                            ins.then_inc(xprobs_ready, 1)
                    ins.then_inc(take(l, f"xs{h}"), 1)
                for h in range(1, XH, 2):
                    act.wait_ge(*full(l, f"xpt{h}"))
                    nc.scalar.activation(xpT[:, h].rearrange("p a s -> p (a s)"), bank(l, f"xpt{h}")[:],
                                         ACT.Copy).then_inc(take(l, f"xpt{h}"), 1)
                for i in range(2):
                    act.wait_ge(*full(l, f"xo{i}"))
                    nc.scalar.activation(zqk[:, 4 + 2 * i:6 + 2 * i, :].rearrange("p a s -> p (a s)"),
                                         bank(l, f"xo{i}")[:], ACT.Copy).then_inc(take(l, f"xo{i}"), 1)

                mean_squares(l, [f"xw{i}" for i in range(4)])
                gained(l, "zT", "ffn")
                if l == 0:
                    for t in range(TT):
                        for i in range(FB):
                            a, b = i * BANK, min(i * BANK + BANK, DFF)
                            act.wait_ge(*full(l, f"g{t}{i}"))
                            nc.scalar.activation(hid[:, t, a:b], bank(l, f"g{t}{i}")[:, 0:b - a],
                                                 ACT.Silu).then_inc(take(l, f"g{t}{i}"), 1)
                    for t in range(TT):
                        for i in range(1, FB, 2):
                            k = min(4, FT - 4 * i)
                            act.wait_ge(*full(l, f"hT{t}{i}"))
                            nc.scalar.activation(hidT[:, t, 4 * i:4 * i + k, :].rearrange("p a s -> p (a s)"),
                                                 bank(l, f"hT{t}{i}")[:, 0:k * P], ACT.Copy).then_inc(take(l, f"hT{t}{i}"), 1)
                else:
                    act.wait_ge(topd_ready, 1)
                    nc.scalar.activation(gw[:, :, 1:2], gw[:, :, 0:1], ACT.Exp).then_inc(tope_ready, 1)

            act.wait_ge(route_ready, 1)
            rounds = act.value_load(npass[0:1, 0:1], min_val=1, max_val=2)
            with act.Fori(0, rounds) as rnd:
                with act.Fori(0, NE) as e:
                    p = rnd * NE + e
                    for i in range(FB):
                        a, b = i * BANK, min(i * BANK + BANK, DFF)
                        act.wait_ge(*lfull(f"g{i}", p))
                        nc.scalar.activation(h1[:, a:b], lbank(f"g{i}")[:, 0:b - a], ACT.Silu).then_inc(ltake(f"g{i}"), 1)
                    for i in range(1, FB, 2):
                        k = min(4, FT - 4 * i)
                        act.wait_ge(*lfull(f"hT{i}", p))
                        nc.scalar.activation(h1T[:, 4 * i:4 * i + k, :].rearrange("p a s -> p (a s)"),
                                             lbank(f"hT{i}")[:, 0:k * P], ACT.Copy).then_inc(ltake(f"hT{i}"), 1)
                    for i in range(2):
                        act.wait_ge(*lfull(f"d{i}", p))
                        nc.scalar.activation(yexp[:, i * BANK:i * BANK + BANK], lbank(f"d{i}")[:],
                                             ACT.Copy).then_inc(ltake(f"d{i}"), 1)

        @block.vector
        def _(dve):
            steps = [0]

            def then_wait(ins):
                steps[0] += 1
                ins.then_inc(dve_step, 1)
                dve.wait_ge(dve_step, steps[0])

            def normalise(l, n, src, at, dst):
                dve.wait_ge(rstd_ready, RSTDS[l, n])
                for t in range(TT):
                    nc.vector.tensor_scalar(dst[:, t, :], src[:, t, :], msq[:, at + t:at + t + 1], None,
                                            ALU.mult).then_inc(xn_ready, 1)

            def refine_rows(l, n, result, y):
                rows = y.shape[0]
                u = newton[0:rows, :]
                if ROWS[l, n] > 1:
                    dve.wait_ge(rows_ready, ROWS[l, n] - 1)
                dve.wait_ge(guess_ready, ROWS[l, n])
                then_wait(nc.vector.tensor_tensor(u, y, y, ALU.mult))
                nc.vector.scalar_tensor_tensor(u, bank(l, result)[0:rows, 0:S], EPS, u, ALU.add, ALU.mult
                                               ).then_inc(take(l, result), 1)
                dve.wait_ge(*taken(l, result))
                then_wait(nc.vector.tensor_scalar(u, u, -0.5, 1.5, ALU.mult, ALU.add))
                nc.vector.tensor_tensor(y, y, u, ALU.mult).then_inc(rows_ready, 1)

            def gained(l, names, gain):
                for i in (0, 2):
                    dve.wait_ge(*full(l, f"{names}{i}"))
                    nc.vector.tensor_tensor(hT[:, 2 * i:2 * i + 2, :], bank(l, f"{names}{i}")[:].rearrange("p (k s) -> p k s", k=2),
                                            bcast_last(col(l, gain, 2 * i, 2), S), ALU.mult).then_inc(take(l, f"{names}{i}"), 1)

            def add_residual(l, names):
                for t in range(TT):
                    for i in range(2):
                        n = f"{names}{2 * t + i}"
                        dve.wait_ge(*full(l, n))
                        xs = xres[:, t, i * BANK:i * BANK + BANK]
                        nc.vector.tensor_tensor(xs, xs, bank(l, n)[:], ALU.add).then_inc(take(l, n), 1)

            for l in range(L):
                if l == 0:
                    dve.wait_ge(*full(0, "vec"))
                    nc.vector.tensor_copy(vcols[:], bank(0, "vec")[:, 0:2 * NV]).then_inc(take(0, "vec"), 1)
                normalise(l, "mix", xres, 0, xn)
                if l == 0:
                    normalise(l, "mem", memraw, 2, memraw)
                    dve.wait_ge(*taken(0, "vec"))
                gained(l, "xT", "mix")
                dve.wait_ge(*full(l, "f"))
                nc.vector.tensor_copy(fz[:, 0, :], bank(l, "f")[:, 0:TT * FH]).then_inc(take(l, "f"), 1)
                dve.wait_ge(*taken(l, "f"))
                then_wait(nc.vector.tensor_scalar(fz[:, 3, :], fz[:, 0, :], 0.0, None, ALU.min))
                nc.vector.scalar_tensor_tensor(fz[:, 1, :], fz[:, 3, :], 2.0, fz[:, 0, :], ALU.mult, ALU.subtract
                                               ).then_inc(fabs_ready, 1)
                dve.wait_ge(fln_ready, l + 1)
                nc.vector.tensor_tensor(fz[:, 3, :], fz[:, 3, :], fz[:, 2, :], ALU.subtract).then_inc(logf_ready, 1)
                if l == 0:
                    for i in range(4):
                        dve.wait_ge(*full(l, f"mT{i}"))
                        nc.vector.tensor_copy(memT[:, 2 * i:2 * i + 2, :].rearrange("p k s -> p (k s)"), bank(l, f"mT{i}")[:]
                                              ).then_inc(take(l, f"mT{i}"), 1)
                for i in range(4):
                    dve.wait_ge(*full(l, f"qk{i}"))
                    nc.vector.tensor_copy(zqk[:, 2 * i:2 * i + 2, :].rearrange("p a s -> p (a s)"), bank(l, f"qk{i}")[:]
                                          ).then_inc(take(l, f"qk{i}"), 1)
                refine_rows(l, "qk", "ssqk", mqk[:])
                for i in range(2):
                    dve.wait_ge(*full(l, f"conv{4 + i}"))
                    dve.wait_ge(*taken(l, f"conv{2 + i}"))
                    u = zc[:, 4 + 2 * i:6 + 2 * i, :].rearrange("p a s -> p (a s)")
                    nc.vector.tensor_tensor(u, bank(l, f"conv{4 + i}")[:], u, ALU.mult).then_inc(take(l, f"conv{4 + i}"), 1)
                for i in range(4):
                    dve.wait_ge(*full(l, f"bq{i}"))
                    qk = zqk[:, 2 * i:2 * i + 2, :].rearrange("p a s -> p (a s)")
                    nc.vector.scalar_tensor_tensor(qk, qk, col(l, "q" if i < 2 else "k"), bank(l, f"bq{i}")[:],
                                                   ALU.mult, ALU.mult).then_inc(take(l, f"bq{i}"), 1)
                for h in range(FH):
                    dve.wait_ge(*full(l, f"s{h}"))
                    nc.vector.scalar_tensor_tensor(sc[:, h, :], bank(l, f"s{h}")[:, 0:3 * P], HD ** -0.5, mask[:],
                                                   ALU.mult, ALU.add).then_inc(take(l, f"s{h}"), 1)
                    if h % 4 == 3:
                        for i in range(4):
                            dve.wait_ge(*taken(l, f"s{h - i}"))
                        for q, (a, b) in enumerate(((0, P), (P, 3 * P))):
                            nc.vector.tensor_reduce(negmax[:, q, h - 3:h + 1], sc[:, h - 3:h + 1, a:b], AX_X, ALU.max,
                                                    negate=True).then_inc(negmax_ready, 1)
                for i in range(2):
                    dve.wait_ge(*taken(l, f"conv{4 + i}"))
                    dve.wait_ge(*taken(l, f"conv{i}"))
                for j in range(4):
                    u, acc, bj = zc[:, 4 + j, :], zc[:, 8 + j, :], zc[:, j, :]
                    then_wait(nc.vector.tensor_scalar(acc, u, col(l, "tap", 8 + j), None, ALU.mult))
                    for back in (1, 2):
                        then_wait(nc.vector.scalar_tensor_tensor(acc[:, back:S], u[:, 0:S - back], col(l, "tap", 8 - 4 * back + j),
                                                                 acc[:, back:S], ALU.mult, ALU.add))
                    ins = nc.vector.tensor_tensor(bj, bj, acc, ALU.mult)
                    if j == 3:
                        ins.then_inc(conv_ready, 1)
                    else:
                        then_wait(ins)
                refine_rows(l, "cv", "ssc", mcv[:])
                refine_rows(l, "mk", "ssmk", mmk[:])
                dve.wait_ge(conv_ready, l + 1)
                for i in range(2):
                    dve.wait_ge(*full(l, f"bc{i}"))
                    for j in (2 * i, 2 * i + 1):
                        ins = nc.vector.scalar_tensor_tensor(yT[:, j, :], zc[:, j, :], col(l, "cv", j),
                                                             bank(l, f"bc{i}")[:, (j % 2) * S:(j % 2) * S + S], ALU.mult, ALU.mult)
                    ins.then_inc(take(l, f"bc{i}"), 1)
                for i in range(2):
                    dve.wait_ge(*full(l, f"bmk{i}"))
                    kk = xk[:, 2 * i:2 * i + 2, :].rearrange("p a s -> p (a s)")
                    nc.vector.scalar_tensor_tensor(kk, kk, col(l, "xk"), bank(l, f"bmk{i}")[:], ALU.mult, ALU.mult
                                                   ).then_inc(take(l, f"bmk{i}"), 1)
                dve.wait_ge(probs_ready, 16 * (l + 1))
                then_wait(nc.vector.reciprocal(denom[:], denom[:]))
                for h in range(0, FH, 2):
                    dve.wait_ge(*full(l, f"pt{h}"))
                    nc.vector.tensor_copy(pT[:, h, :], bank(l, f"pt{h}")[:, 0:3 * P]).then_inc(take(l, f"pt{h}"), 1)
                for q in range(2):
                    dve.wait_ge(*full(l, f"o{q}"))
                    nc.vector.tensor_tensor(otok[:, q, :].rearrange("p (h d) -> p h d", h=FH),
                                            bank(l, f"o{q}")[:].rearrange("p (h d) -> p h d", h=FH),
                                            bcast_last(denom[:, q, :], HD), ALU.mult).then_inc(take(l, f"o{q}"), 1)
                dve.wait_ge(squares_ready, SQUARES[l, "fox"])
                nc.vector.tensor_reduce(mfox[:], osq, AX_X, ALU.add).then_inc(osum_ready, 1)
                dve.wait_ge(rstd_ready, RSTDS[l, "fox"])
                ot = otok.rearrange("p t (h d) -> p (t h) d", d=HD)
                nc.vector.tensor_tensor(ot, ot, bcast_last(mfox[:], HD), ALU.mult).then_inc(onorm_ready, 1)
                for i in range(2):
                    dve.wait_ge(*full(l, f"oT{i}"))
                    nc.vector.tensor_tensor(yT[:, 4 + 2 * i:6 + 2 * i, :], bank(l, f"oT{i}")[:].rearrange("p (k s) -> p k s", k=2),
                                            bcast_last(col(l, "fox", 2 * i, 2), S), ALU.mult).then_inc(take(l, f"oT{i}"), 1)
                add_residual(l, "wo")

                normalise(l, "xa", xres, 0, xn)
                gained(l, "yT", "xa")
                for i in range(2):
                    dve.wait_ge(*full(l, f"xq{i}"))
                    nc.vector.tensor_copy(zqk[:, 2 * i:2 * i + 2, :].rearrange("p a s -> p (a s)"), bank(l, f"xq{i}")[:]
                                          ).then_inc(take(l, f"xq{i}"), 1)
                refine_rows(l, "xq", "ssxq", mxq[:])
                for i in range(2):
                    dve.wait_ge(*full(l, f"bxq{i}"))
                    qq = zqk[:, 2 * i:2 * i + 2, :].rearrange("p a s -> p (a s)")
                    nc.vector.scalar_tensor_tensor(qq, qq, col(l, "xq"), bank(l, f"bxq{i}")[:], ALU.mult, ALU.mult
                                                   ).then_inc(take(l, f"bxq{i}"), 1)
                for h in range(XH):
                    dve.wait_ge(*full(l, f"xs{h}"))
                    then_wait(nc.vector.tensor_reduce(xnm[:, h, :], bank(l, f"xs{h}")[:].rearrange("p (q m) -> p q m", q=2),
                                                      AX_X, ALU.max, negate=True))
                    nc.vector.tensor_scalar(xnm[:, h, :], xnm[:, h, :], XHD ** -0.5, None, ALU.mult).then_inc(xmax_ready, 1)
                for h in range(XH):
                    dve.wait_ge(*taken(l, f"xs{h}"))
                    dve.wait_ge(xprobs_ready, XH * l + h + 1)
                    then_wait(nc.vector.reciprocal(xden[:, h, :], xden[:, h, :]))
                    nc.vector.tensor_tensor(xsc[:, h], xsc[:, h], bcast_last(xden[:, h, :], S), ALU.mult).then_inc(xpn_ready, 1)
                for h in range(0, XH, 2):
                    dve.wait_ge(*full(l, f"xpt{h}"))
                    nc.vector.tensor_copy(xpT[:, h].rearrange("p a s -> p (a s)"), bank(l, f"xpt{h}")[:]
                                          ).then_inc(take(l, f"xpt{h}"), 1)
                add_residual(l, "xw")

                normalise(l, "ffn", xres, 0, xn)
                gained(l, "zT", "ffn")
                if l == 0:
                    for t in range(TT):
                        for i in range(FB):
                            a, b = i * BANK, min(i * BANK + BANK, DFF)
                            dve.wait_ge(*full(l, f"u{t}{i}"))
                            dve.wait_ge(*taken(l, f"g{t}{i}"))
                            nc.vector.tensor_tensor(hid[:, t, a:b], bank(l, f"u{t}{i}")[:, 0:b - a], hid[:, t, a:b],
                                                    ALU.mult).then_inc(take(l, f"u{t}{i}"), 1)
                    for t in range(TT):
                        for i in range(0, FB, 2):
                            k = min(4, FT - 4 * i)
                            dve.wait_ge(*full(l, f"hT{t}{i}"))
                            nc.vector.tensor_copy(hidT[:, t, 4 * i:4 * i + k, :].rearrange("p a s -> p (a s)"),
                                                  bank(l, f"hT{t}{i}")[:, 0:k * P]).then_inc(take(l, f"hT{t}{i}"), 1)
                        for i in range(2):
                            dve.wait_ge(*full(l, f"d{t}{i}"))
                            xs = xres[:, t, i * BANK:i * BANK + BANK]
                            nc.vector.tensor_tensor(xs, xs, bank(l, f"d{t}{i}")[:], ALU.add).then_inc(take(l, f"d{t}{i}"), 1)

            l = L - 1
            dve.wait_ge(*full(l, "r"))
            nc.vector.tensor_copy(logit[:].rearrange("p t e -> p (t e)"), bank(l, "r")[:, 0:TT * NE]).then_inc(take(l, "r"), 1)
            dve.wait_ge(*taken(l, "r"))
            for t in range(TT):
                then_wait(nc.vector.max(top[:, t, :], logit[:, t, :]))
                then_wait(nc.vector.max_index(topi[:, t, :], top[:, t, :], logit[:, t, :]))
            nc.vector.tensor_tensor(gw[:, :, 0:1], top[:, :, 1:2], top[:, :, 0:1], ALU.subtract).then_inc(topd_ready, 1)
            then_wait(nc.vector.tensor_copy(topf[:], topi[:]))
            for t in range(TT):
                for c in range(2):
                    then_wait(nc.vector.tensor_scalar(hot[:, t, c, :], eight[:], topf[:, t, c:c + 1], None, ALU.is_equal))
            then_wait(nc.vector.memset(pos[:], -1.0))
            then_wait(nc.vector.memset(gates[:], 0.0))
            nc.vector.tensor_tensor(hot[:, :, 2, :], hot[:, :, 0, :], hot[:, :, 1, :], ALU.add).then_inc(sel_ready, 1)
            dve.wait_ge(tope_ready, 1)
            then_wait(nc.vector.tensor_scalar(gw[:, :, 2:3], gw[:, :, 1:2], 1.0, None, ALU.add))
            then_wait(nc.vector.reciprocal(gw[:, :, 2:3], gw[:, :, 2:3]))
            then_wait(nc.vector.tensor_tensor(gw[:, :, 3:4], gw[:, :, 1:2], gw[:, :, 2:3], ALU.mult))
            for t in range(TT):
                then_wait(nc.vector.tensor_scalar(gates[:, t, 0:NE], hot[:, t, 0, :], gw[:, t, 2:3], None, ALU.mult))
                then_wait(nc.vector.scalar_tensor_tensor(gates[:, t, 0:NE], hot[:, t, 1, :], gw[:, t, 3:4], gates[:, t, 0:NE],
                                                         ALU.mult, ALU.add))
            then_wait(nc.vector.tensor_copy(gates[:, :, NE:2 * NE], gates[:, :, 0:NE]))
            dve.wait_ge(sel_ready, 1)
            dve.wait_ge(*full(l, "rank0"))
            nc.vector.scalar_tensor_tensor(pos[:, :, 0:NE], bank(l, "rank0")[:, 0:TT * NE].rearrange("p (t e) -> p t e", t=TT),
                                           1.0 / 8, hot[:, :, 2, :], ALU.mult, ALU.mult).then_inc(take(l, "rank0"), 1)
            dve.wait_ge(*taken(l, "rank0"))
            then_wait(nc.vector.tensor_scalar(pos[:, :, 0:NE], pos[:, :, 0:NE], -1.0, None, ALU.add))
            then_wait(nc.vector.tensor_scalar(pos[:, :, NE:2 * NE], pos[:, :, 0:NE], -float(PASS_CAP), None, ALU.add))
            dve.wait_ge(*full(l, "rank1"))
            nc.vector.tensor_reduce(cnt[0:1, 0:1], bank(l, "rank1")[0:1, 0:NE], AX_X, ALU.max).then_inc(take(l, "rank1"), 1)
            dve.wait_ge(*taken(l, "rank1"))
            nc.vector.tensor_scalar(npass[0:1, 0:1], cnt[0:1, 0:1], 8.0 * PASS_CAP, 1.0, ALU.is_gt, ALU.add
                                    ).then_inc(route_ready, 1)

            def hot_places(idx):
                for t in range(TT):
                    ins = nc.vector.tensor_scalar(oneh[:, t, :], place[:], pos[:, t, idx], None, ALU.is_equal)
                ins.then_inc(oneh_ready, 1)

            hot_places(slice(0, 1))
            for i in range(2):
                dve.wait_ge(*full(l, f"ga{i}"))
                nc.vector.tensor_tensor(xg[:, 4 * i:4 * i + 4, :], bank(l, f"ga{i}")[:].rearrange("p (k s) -> p k s", k=4),
                                        bcast_last(col(l, "ffn", 4 * i, 4), PASS_CAP), ALU.mult).then_inc(take(l, f"ga{i}"), 1)

            dve.wait_ge(route_ready, 1)
            rounds = dve.value_load(npass[0:1, 0:1], min_val=1, max_val=2)
            with dve.Fori(0, rounds) as rnd:
                with dve.Fori(0, NE) as e:
                    p = rnd * NE + e
                    hot_places(bass.ds(p + 1, 1))
                    for t in range(TT):
                        ins = nc.vector.tensor_scalar(gated[:, t, :], place[:], pos[:, t, bass.ds(p, 1)], gates[:, t, bass.ds(p, 1)],
                                                      ALU.is_equal, ALU.mult)
                    ins.then_inc(gated_ready, 1)
                    for i in range(FB):
                        a, b = i * BANK, min(i * BANK + BANK, DFF)
                        dve.wait_ge(*lfull(f"u{i}", p))
                        dve.wait_ge(*ltaken(f"g{i}", p))
                        nc.vector.tensor_tensor(h1[:, a:b], lbank(f"u{i}")[:, 0:b - a], h1[:, a:b], ALU.mult
                                                ).then_inc(ltake(f"u{i}"), 1)
                    dve.wait_ge(*lfull("GT", p))
                    nc.vector.tensor_copy(gatedT, lbank("GT")[:, 0:S]).then_inc(ltake("GT"), 1)
                    for i in range(0, FB, 2):
                        k = min(4, FT - 4 * i)
                        dve.wait_ge(*lfull(f"hT{i}", p))
                        nc.vector.tensor_copy(h1T[:, 4 * i:4 * i + k, :].rearrange("p a s -> p (a s)"),
                                              lbank(f"hT{i}")[:, 0:k * P]).then_inc(ltake(f"hT{i}"), 1)
                    for i in range(2):
                        dve.wait_ge(*lfull(f"ga{i}", p))
                        nc.vector.tensor_tensor(xg[:, 4 * i:4 * i + 4, :], lbank(f"ga{i}")[:].rearrange("p (k s) -> p k s", k=4),
                                                bcast_last(col(l, "ffn", 4 * i, 4), PASS_CAP), ALU.mult).then_inc(ltake(f"ga{i}"), 1)
                    for t in range(TT):
                        for i in range(2):
                            dve.wait_ge(*lfull(f"sc{2 * t + i}", p))
                            xs = xres[:, t, i * BANK:i * BANK + BANK]
                            nc.vector.tensor_tensor(xs, xs, lbank(f"sc{2 * t + i}")[:], ALU.add
                                                    ).then_inc(ltake(f"sc{2 * t + i}"), 1)

        @block.tensor
        def _(pe):
            def open_bank(l, n):
                b, use = plan.at[l, n]
                if use > 0:
                    pe.wait_ge(psum_taken[b], use)
                return psum[b]

            def lopen(n, p):
                pe.wait_ge(psum_taken[in_pass.at[n][0]], lcount(n, p))
                return lbank(n)

            def done(l, n):
                return psum_full[plan.at[l, n][0]]

            def ldone(n):
                return psum_full[in_pass.at[n][0]]

            def weights(*name):
                n = fill_at[name]
                pe.wait_ge(slot_filled[n % NSLOT], 16 * (n // NSLOT + 1))
                k, c = fills[n][1]
                return ring[:, n % NSLOT, 0:k * c].rearrange("p (k c) -> p k c", k=k)

            def expert_weights(j, p):
                slot = (NSTATIC + j) % NSLOT
                pe.wait_ge(slot_filled[slot], p * (16 * (PASS_FILLS // NSLOT)) + 16 * ((NSTATIC + j) // NSLOT + 1))
                return ring[:, slot, :]

            def mm(dst, lhsT, rhs, first, last):
                return nc.tensor.matmul(dst, lhsT, rhs, start=first, stop=last)

            def transposed(l, names, src):
                for i in range(4):
                    ps = open_bank(l, f"{names}{i}")
                    for k in range(2):
                        for t in range(TT):
                            c = (2 * i + k) * P
                            ins = nc.tensor.transpose(ps[:, k * S + t * P:k * S + t * P + P], src[:, t, c:c + P], ident[:])
                    ins.then_inc(done(l, f"{names}{i}"), 1)

            def hT_ready(l, names):
                for i in range(4):
                    pe.wait_ge(*taken(l, f"{names}{i}"))

            def channel_tile(ps, w, rhs):
                for k in range(KT):
                    ins = mm(ps, w[:, k, :], rhs[:, k, :], k == 0, k == KT - 1)
                return ins

            def logits(l, n, w, bias):
                ps = open_bank(l, n)
                for t in range(TT):
                    for k in range(KT):
                        mm(ps[:, 8 * t:8 * t + 8], hT[:, k, t * P:t * P + P], w[:, k, :], k == 0, False)
                    ins = mm(ps[:, 8 * t:8 * t + 8], ones1[:], bias, False, True)
                ins.then_inc(done(l, n), 1)

            def mean_rows(l, n, sel, at, width, src, tiles):
                ps = open_bank(l, n)
                for j in range(tiles):
                    step = at - (2 * j if width != 4 else j)
                    ins = mm(ps[0:width, 0:S], sel[:, step:step + width], src[:, j, :], j == 0, j == tiles - 1)
                ins.then_inc(done(l, n), 1)

            def spread_rows(l, names, spread, rows, tiles):
                for i in range(tiles // 2):
                    ps = open_bank(l, f"{names}{i}")
                    for k in range(2):
                        c = (2 * i + k) * P
                        ins = mm(ps[:, k * S:k * S + S], spread[:, c:c + P], rows, True, True)
                    ins.then_inc(done(l, f"{names}{i}"), 1)

            def gather(open_, done_):
                for i in range(2):
                    ps = open_(f"ga{i}")
                    for k in range(4):
                        c = (4 * i + k) * P
                        for t in range(TT):
                            ins = mm(ps[:, k * P:k * P + P], xn[:, t, c:c + P], oneh[:, t, :], t == 0, t == TT - 1)
                    ins.then_inc(done_(f"ga{i}"), 1)

            def bank_cols(i):
                return i * BANK, min(i * BANK + BANK, DFF)

            pe.wait_ge(ident_ready, 1)
            pe.wait_ge(params_loaded, 16 * NPARAMS)
            ps = open_bank(0, "vec")
            nc.tensor.transpose(ps[:, 0:2 * NV], vrows[:], ident[0:2 * NV, 0:2 * NV]).then_inc(done(0, "vec"), 1)
            for l in range(L):
                pe.wait_ge(xn_ready, XN[l, "mix"])
                transposed(l, "xT", xn)
                hT_ready(l, "xT")
                if l == 0:
                    pe.wait_ge(consts_ready, 1)
                logits(l, "f", wf[:, l], brow[0:1, l * FH:l * FH + FH])
                if l == 0:
                    pe.wait_ge(xn_ready, XN[0, "mem"])
                    transposed(0, "mT", memraw)
                for i in range(4):
                    ps = open_bank(l, f"qk{i}")
                    for c in (2 * i, 2 * i + 1):
                        w = weights(l, "z", c // 3)
                        ins = channel_tile(ps[:, (c % 2) * S:(c % 2) * S + S], w[:, :, (c % 3) * P:(c % 3) * P + P], hT)
                    ins.then_inc(done(l, f"qk{i}"), 1)
                for t in range(TT):
                    ps = open_bank(l, f"v{t}")
                    for s, (a, b) in ((2, (2 * P, 3 * P)), (3, (0, 3 * P))):
                        w = weights(l, "z", s)
                        at = 0 if s == 2 else P
                        for k in range(KT):
                            ins = mm(ps[:, at:at + b - a], hT[:, k, t * P:t * P + P], w[:, k, a:b], k == 0, k == KT - 1)
                    ins.then_inc(done(l, f"v{t}"), 1)
                pe.wait_ge(squares_ready, SQUARES[l, "qk3"])
                mean_rows(l, "ssqk", selg, 14, 16, sq, 8)
                for i in range(6):
                    ps = open_bank(l, f"conv{i}")
                    for c in (2 * i, 2 * i + 1):
                        w = weights(l, "z", 4 + c // 3)
                        ins = channel_tile(ps[:, (c % 2) * S:(c % 2) * S + S], w[:, :, (c % 3) * P:(c % 3) * P + P], hT)
                    ins.then_inc(done(l, f"conv{i}"), 1)
                pe.wait_ge(rows_ready, ROWS[l, "qk"])
                spread_rows(l, "bq", spreadg[:], mqk[:], 8)
                pe.wait_ge(decay_ready, l + 1)
                for i in range(4):
                    pe.wait_ge(*taken(l, f"bq{i}"))
                for h in range(FH):
                    r, j = (h % 2) * HD, h // 2
                    q, k = zqk[r:r + HD, j, :], zqk[r:r + HD, 4 + j, :]
                    ps = open_bank(l, f"s{h}")
                    mm(ps[:, 0:P], q[:, 0:P], k[:, 0:P], True, False)
                    mm(ps[:, 0:P], decay[:, h, 0:P], after[:, 0:P], False, True)
                    mm(ps[:, P:3 * P], q[:, P:S], k, True, False)
                    mm(ps[:, P:2 * P], decay[:, h, P:S], after[:, 0:P], False, False)
                    mm(ps[:, P:3 * P], decay[:, h, S:3 * P], after[:, P:3 * P], False, True).then_inc(done(l, f"s{h}"), 1)
                pe.wait_ge(memg_ready, l + 1)
                for i in range(2):
                    ps = open_bank(l, f"mk{i}")
                    w = weights(l, "xkv", i)
                    for c in range(2):
                        ins = channel_tile(ps[:, c * S:c * S + S], w[:, :, c * P:c * P + P], hT)
                    ins.then_inc(done(l, f"mk{i}"), 1)
                for t in range(TT):
                    ps = open_bank(l, f"mv{t}")
                    for s in range(2):
                        w = weights(l, "xkv", 2 + s)
                        for k in range(KT):
                            ins = mm(ps[:, 256 * s:256 * s + 256], hT[:, k, t * P:t * P + P], w[:, k, :], k == 0, k == KT - 1)
                    ins.then_inc(done(l, f"mv{t}"), 1)
                pe.wait_ge(squares_ready, SQUARES[l, "cv"])
                mean_rows(l, "ssc", selg, 14, 8, zc[:, 4:8, :], 4)
                mean_rows(l, "ssmk", selh, 3, 4, ksq, XH)
                pe.wait_ge(rows_ready, ROWS[l, "cv"])
                spread_rows(l, "bc", spreadg[0:8, :], mcv[:], 4)
                pe.wait_ge(rows_ready, ROWS[l, "mk"])
                spread_rows(l, "bmk", spreadh[:], mmk[:], XH)
                for h in range(FH):
                    pe.wait_ge(probs_ready, 2 * FH * l + 2 * h + 2)
                    ps = open_bank(l, f"pt{h}")
                    for c in range(3):
                        ins = nc.tensor.transpose(ps[:, c * P:c * P + P], sc[:, h, c * P:c * P + P], ident[:])
                    ins.then_inc(done(l, f"pt{h}"), 1)
                for t in range(TT):
                    pe.wait_ge(*taken(l, f"v{t}"))
                for q in range(2):
                    ps = open_bank(l, f"o{q}")
                    for h in range(FH):
                        if q == 0:
                            pe.wait_ge(*taken(l, f"pt{h}"))
                        for t in range(q + 1):
                            c = (q + t) * P
                            ins = mm(ps[:, h * HD:h * HD + HD], pT[:, h, c:c + P], vtok[:, t, h * HD:h * HD + HD], t == 0, t == q)
                    ins.then_inc(done(l, f"o{q}"), 1)
                pe.wait_ge(onorm_ready, l + 1)
                for i in range(2):
                    ps = open_bank(l, f"oT{i}")
                    for k in range(2):
                        for t in range(TT):
                            c = (2 * i + k) * P
                            ins = nc.tensor.transpose(ps[:, k * S + t * P:k * S + t * P + P], otok[:, t, c:c + P], ident[:])
                    ins.then_inc(done(l, f"oT{i}"), 1)
                def token_projection(names, fill, rows, per_slot, src, waits):
                    banks = [open_bank(l, f"{names}{i}") for i in range(4)]
                    for k in range(rows):
                        w = weights(l, fill, k // per_slot)
                        for n in waits.get(k, ()):
                            pe.wait_ge(*taken(l, n))
                        for i in range(4):
                            t, half = i // 2, i % 2
                            ins = mm(banks[i][:], src[:, k, t * P:t * P + P], w[:, k % per_slot, half * BANK:half * BANK + BANK],
                                     k == 0, k == rows - 1)
                            if k == rows - 1:
                                ins.then_inc(done(l, f"{names}{i}"), 1)
                        if k < rows - 1 and k % per_slot == per_slot - 1:
                            ins.then_inc(slots_used, 1)

                token_projection("wo", "wo", KT, 2, yT, {0: ("bc0", "bc1"), 4: ("oT0", "oT1")})

                pe.wait_ge(xn_ready, XN[l, "xa"])
                transposed(l, "yT", xn)
                hT_ready(l, "yT")
                for i in range(2):
                    ps = open_bank(l, f"xq{i}")
                    w = weights(l, "xq", i)
                    for c in range(2):
                        ins = channel_tile(ps[:, c * S:c * S + S], w[:, :, c * P:c * P + P], hT)
                    ins.then_inc(done(l, f"xq{i}"), 1)
                pe.wait_ge(squares_ready, SQUARES[l, "xq"])
                mean_rows(l, "ssxq", selh, 3, 4, sq, XH)
                pe.wait_ge(rows_ready, ROWS[l, "xq"])
                spread_rows(l, "bxq", spreadh[:], mxq[:], XH)
                for i in range(2):
                    pe.wait_ge(*taken(l, f"bmk{i}"))
                for h in range(XH):
                    ps = open_bank(l, f"xs{h}")
                    pe.wait_ge(*taken(l, f"bxq{h // 2}"))
                    for q in range(2):
                        ins = mm(ps[:, q * S:q * S + S], zqk[:, h, q * P:q * P + P], xk[:, h, :], True, True)
                    ins.then_inc(done(l, f"xs{h}"), 1)
                for h in range(XH):
                    ps = open_bank(l, f"xpt{h}")
                    pe.wait_ge(xpn_ready, XH * l + h + 1)
                    for m in range(2):
                        for q in range(2):
                            ins = nc.tensor.transpose(ps[:, m * S + q * P:m * S + q * P + P], xsc[:, h, q, m * P:m * P + P], ident[:])
                    ins.then_inc(done(l, f"xpt{h}"), 1)
                for t in range(TT):
                    pe.wait_ge(*taken(l, f"mv{t}"))
                for i in range(2):
                    ps = open_bank(l, f"xo{i}")
                    for h in (2 * i, 2 * i + 1):
                        pe.wait_ge(*taken(l, f"xpt{h}"))
                        for m in range(2):
                            ins = mm(ps[:, (h % 2) * S:(h % 2) * S + S], xv[:, m, h * XHD:h * XHD + XHD], xpT[:, h, m, :], m == 0, m == 1)
                    ins.then_inc(done(l, f"xo{i}"), 1)
                token_projection("xw", "xo", XH, 2, zqk[:, 4:8, :], {0: ("xo0",), 2: ("xo1",)})

                pe.wait_ge(xn_ready, XN[l, "ffn"])
                transposed(l, "zT", xn)
                hT_ready(l, "zT")
                if l == 0:
                    for part_ in ("g", "u"):
                        for t in range(TT):
                            for k in range(KT):
                                w = weights(l, part_, k)
                                for i in range(FB):
                                    a, b = bank_cols(i)
                                    n = f"{part_}{t}{i}"
                                    ps = open_bank(l, n) if k == 0 else bank(l, n)
                                    ins = mm(ps[:, 0:b - a], hT[:, k, t * P:t * P + P], w[:, 0, a:b], k == 0, k == KT - 1)
                                    if k == KT - 1:
                                        ins.then_inc(done(l, n), 1)
                                if t == TT - 1 and k < KT - 1:
                                    ins.then_inc(slots_used, 1)
                    for t in range(TT):
                        for i in range(FB):
                            pe.wait_ge(*taken(l, f"u{t}{i}"))
                            ps = open_bank(l, f"hT{t}{i}")
                            for j in range(4 * i, min(4 * i + 4, FT)):
                                ins = nc.tensor.transpose(ps[:, (j % 4) * P:(j % 4) * P + P], hid[:, t, j * P:j * P + P], ident[:])
                            ins.then_inc(done(l, f"hT{t}{i}"), 1)
                        banks = [open_bank(l, f"d{t}{i}") for i in range(2)]
                        for j in range(FT):
                            if j % 4 == 0:
                                pe.wait_ge(*taken(l, f"hT{t}{j // 4}"))
                            w = weights(l, "d", j // DROWS)
                            for i in range(2):
                                ins = mm(banks[i][:], hidT[:, t, j, :], w[:, j % DROWS, i * BANK:i * BANK + BANK], j == 0, j == FT - 1)
                                if j == FT - 1:
                                    ins.then_inc(done(l, f"d{t}{i}"), 1)
                            if t == TT - 1 and j < FT - 1 and j % DROWS == DROWS - 1:
                                ins.then_inc(slots_used, 1)

            l = L - 1
            logits(l, "r", wr[:], brow[0:1, L * FH:L * FH + NE])
            pe.wait_ge(sel_ready, 1)
            ps = open_bank(l, "rank0")
            mm(ps[:, 0:NE], tri8[:, 0:P], hot[:, 0, 2, :], True, True)
            mm(ps[:, NE:2 * NE], tri8[:, P:S], hot[:, 0, 2, :], True, False)
            mm(ps[:, NE:2 * NE], tri8[:, 0:P], hot[:, 1, 2, :], False, True).then_inc(done(l, "rank0"), 1)
            ps = open_bank(l, "rank1")
            mm(ps[0:1, 0:NE], tri8[:, P:P + 1], hot[:, 0, 2, :], True, False)
            mm(ps[0:1, 0:NE], tri8[:, P:P + 1], hot[:, 1, 2, :], False, True).then_inc(done(l, "rank1"), 1)
            pe.wait_ge(oneh_ready, 1)
            gather(lambda n: open_bank(l, n), lambda n: done(l, n))
            for i in range(2):
                pe.wait_ge(*taken(l, f"ga{i}"))

            pe.wait_ge(route_ready, 1)
            rounds = pe.value_load(npass[0:1, 0:1], min_val=1, max_val=2)
            with pe.Fori(0, rounds) as rnd:
                with pe.Fori(0, NE) as e:
                    p = rnd * NE + e
                    for half, names in enumerate(("g", "u")):
                        for k in range(KT):
                            w = expert_weights(half * KT + k, p)
                            for i in range(FB):
                                a, b = bank_cols(i)
                                ps = lopen(f"{names}{i}", p) if k == 0 else lbank(f"{names}{i}")
                                ins = mm(ps[:, 0:b - a], xg[:, k, :], w[:, a:b], k == 0, k == KT - 1)
                                if k == KT - 1:
                                    ins.then_inc(ldone(f"{names}{i}"), 1)
                            if k < KT - 1:
                                ins.then_inc(slots_used, 1)
                    pe.wait_ge(gated_ready, p + 1)
                    ps = lopen("GT", p)
                    for t in range(TT):
                        ins = nc.tensor.transpose(ps[:, t * P:t * P + P], gated[:, t, :], ident[:])
                    ins.then_inc(ldone("GT"), 1)
                    for i in range(FB):
                        pe.wait_ge(*ltaken(f"u{i}", p))
                        ps = lopen(f"hT{i}", p)
                        for j in range(4 * i, min(4 * i + 4, FT)):
                            ins = nc.tensor.transpose(ps[:, (j % 4) * P:(j % 4) * P + P], h1[:, j * P:j * P + P], ident[:])
                        ins.then_inc(ldone(f"hT{i}"), 1)
                    banks = [lopen(f"d{i}", p) for i in range(2)]
                    for j in range(FT):
                        if j % 4 == 0:
                            pe.wait_ge(*ltaken(f"hT{j // 4}", p))
                        if j % DROWS == 0:
                            w = expert_weights(2 * KT + j // DROWS, p)
                        for i in range(2):
                            c = (j % DROWS) * D + i * BANK
                            ins = mm(banks[i][:], h1T[:, j, :], w[:, c:c + BANK], j == 0, j == FT - 1)
                            if j == FT - 1:
                                ins.then_inc(ldone(f"d{i}"), 1)
                        if j < FT - 1 and j % DROWS == DROWS - 1:
                            ins.then_inc(slots_used, 1)
                    pe.wait_ge(oneh_ready, p + 2)
                    gather(lambda n: lopen(n, p), ldone)
                    pe.wait_ge(*ltaken("GT", p))
                    for t in range(TT):
                        for i in range(2):
                            ps = lopen(f"sc{2 * t + i}", p)
                            pe.wait_ge(*ltaken(f"d{i}", p))
                            mm(ps[:], gatedT[:, t * P:t * P + P], yexp[:, i * BANK:i * BANK + BANK], True, True
                               ).then_inc(ldone(f"sc{2 * t + i}"), 1)
                    for i in range(2):
                        pe.wait_ge(*ltaken(f"ga{i}", p))


_INS = ['x', 'mem', 'g_mix', 'w_in', 'conv_w', 'b_f', 'g_q', 'g_k', 'g_conv_out', 'g_fox_out', 'w_out',
        'g_xa', 'g_mem', 'w_xq', 'w_xkv', 'g_xq', 'g_xk', 'w_xo', 'g_ffn', 'w_gate', 'w_up', 'w_down',
        'w_router', 'b_router', 'we_gate', 'we_up', 'we_down']


def kernel(**inputs):
    import concourse.bacc as bacc
    from concourse.bass_utils import run_bass_kernel_spmd

    nc = bacc.Bacc("TRN2", target_bir_lowering=False, num_devices=1)
    arrays, args = {}, []
    for name in _INS:
        a = np.ascontiguousarray(inputs[name])
        arrays[f"in_{name}"] = a
        args.append(nc.dram_tensor(f"in_{name}", a.shape, mybir.dt.from_np(a.dtype), kind="ExternalInput").ap())
    out = nc.dram_tensor("out_x", arrays["in_x"].shape, F32, kind="ExternalOutput").ap()
    build(nc, *args, out)
    r = run_bass_kernel_spmd(nc, [arrays], core_ids=[0])
    return r.results[0]["out_x"]
```

```python
from contextlib import ExitStack

import numpy as np

import concourse.bass as bass
from concourse import mybir

P = 128
F32 = mybir.dt.float32
F32R = mybir.dt.float32r
I32 = mybir.dt.int32
U32 = mybir.dt.uint32
ALU = mybir.AluOpType
ACT = mybir.ActivationFunctionType
AX_X = mybir.AxisListType.X

EPS = 1e-6
HD = 64
XHD = 128
MASKED = -3.0e38
BANK = 512
NBANK = 8
NSLOT = 4
SLOT = 3072
ZCOLS = SLOT // 8
PASS_CAP = 128


def bcast_last(ap, n):
    return ap.unsqueeze(len(ap.shape)).to_broadcast([*ap.shape, n])


class PsumPlan:

    def __init__(self):
        self.at, self.uses, self.turn = {}, [0] * NBANK, 0

    def add(self, name):
        b = self.turn % NBANK
        self.turn += 1
        self.at[name] = (b, self.uses[b])
        self.uses[b] += 1


def layer_results(layer):
    names = [f"xT{i}" for i in range(4)] + ["f"]
    if layer == 0:
        names += [f"mT{i}" for i in range(4)]
    names += [f"qk{i}" for i in range(4)] + ["v0", "v1", "ssqk"]
    names += [f"conv{i}" for i in range(6)] + [f"bq{i}" for i in range(4)]
    names += [f"s{h}" for h in range(8)]
    names += ["mk0", "mk1", "mv0", "mv1", "ssc", "ssmk"] + [f"pt{h}" for h in range(4)]
    names += ["bc0", "bc1", "bmk0", "bmk1"] + [f"pt{h}" for h in range(4, 8)] + ["o0", "o1"]
    names += [f"wo{i}" for i in range(4)] + ["oT0", "oT1"]
    names += [f"yT{i}" for i in range(4)] + ["xq0", "xq1", "ssxq", "bxq0", "bxq1"]
    names += [f"xs{h}" for h in range(4)] + [f"xpt{h}" for h in range(4)] + ["xo0", "xo1"]
    names += [f"xw{i}" for i in range(4)] + [f"zT{i}" for i in range(4)]
    return names


def build(nc, x, mem, g_mix, w_in, conv_w, b_f, g_q, g_k, g_conv_out, g_fox_out, w_out,
          g_xa, g_mem, w_xq, w_xkv, g_xq, g_xk, w_xo, g_ffn, w_gate, w_up, w_down,
          w_router, b_router, we_gate, we_up, we_down, out):
    L, D, ICOLS = w_in.shape
    _, S, _ = x.shape
    DFF = w_gate.shape[2]
    NE = we_gate.shape[1]
    KT = D // P
    TT = S // P
    CC = conv_w.shape[2]
    FH = b_f.shape[1]
    XH = w_xo.shape[1] // XHD
    FT = DFF // P
    FB = -(-DFF // BANK)
    DROWS = SLOT // D
    DSLOT = -(-FT // DROWS)
    HALF = DFF // 2
    HB = -(-HALF // BANK)
    HT = FT // 2
    HSLOT = -(-HT // DROWS)
    assert (L, KT, TT, FH, XH, mem.shape[1]) == (2, 8, 2, 8, 4, S)

    plan = PsumPlan()
    plan.add((0, "vec"))
    for l in range(L):
        for n in layer_results(l):
            plan.add((l, n))
        if l == 0:
            for half in range(2):
                for n in ([f"g{half}{t}{i}" for t in range(TT) for i in range(HB)]
                          + [f"u{half}{t}{i}" for t in range(TT) for i in range(HB)]
                          + [f"hT{half}{i}" for i in range(-(-HT // 2))]
                          + [f"d{half}{t}{i}" for t in range(TT) for i in range(2)]):
                    plan.add((l, n))
        else:
            for n in ["r", "rank0", "rank1", "ga0", "ga1"]:
                plan.add((l, n))
    loop_base, start_turn = list(plan.uses), plan.turn
    pass_names = ([f"g{i}" for i in range(FB)] + [f"u{i}" for i in range(FB)] + ["GT"]
                  + [f"hT{i}" for i in range(FB)] + ["ga0", "ga1", "d0", "d1"] + [f"sc{i}" for i in range(4)])
    in_pass = PsumPlan()
    in_pass.turn = start_turn
    for n in pass_names:
        in_pass.add(n)

    fills = []
    fill_at = {}

    def add_fill(name, src, shape):
        fill_at[name] = len(fills)
        fills.append((src, shape))

    def z_src(l, c0):
        return w_in[l][:, c0:c0 + ZCOLS].rearrange("(k p) c -> p k c", p=P)

    for l in range(L):
        for s in range(8):
            add_fill((l, "z", s), z_src(l, (3 * CC + ZCOLS * s) if s < 4 else ZCOLS * (s - 4)), (KT, ZCOLS))
        for s in range(4):
            add_fill((l, "xkv", s), w_xkv[l][:, 256 * s:256 * s + 256].rearrange("(k p) c -> p k c", p=P), (KT, 256))
        for s in range(4):
            add_fill((l, "wo", s), w_out[l][256 * s:256 * s + 256].rearrange("(k p) c -> p k c", p=P), (2, D))
        for s in range(2):
            add_fill((l, "xq", s), w_xq[l][:, 256 * s:256 * s + 256].rearrange("(k p) c -> p k c", p=P), (KT, 256))
        for s in range(2):
            add_fill((l, "xo", s), w_xo[l][256 * s:256 * s + 256].rearrange("(k p) c -> p k c", p=P), (2, D))
        if l == 0:
            for half in range(2):
                c0 = half * HALF
                for nm, w in (("g", w_gate), ("u", w_up)):
                    for k in range(0, KT, 2):
                        add_fill((l, nm, half, k // 2), w[0][P * k:P * k + 2 * P, c0:c0 + HALF].rearrange("(k p) c -> p k c", p=P),
                                 (2, HALF))
                for s in range(HSLOT):
                    k, r0 = min(DROWS, HT - DROWS * s), c0 + P * DROWS * s
                    add_fill((l, "d", half, s), w_down[0][r0:r0 + P * k].rearrange("(k p) c -> p k c", p=P), (k, D))
    NSTATIC = len(fills)
    frees = {}
    for l in range(L):
        for s, n in ((1, "qk2"), (3, "v1"), (5, "conv2"), (7, "conv5")):
            frees[l, "z", s] = n
        for s, n in ((0, "mk0"), (1, "mk1"), (3, "mv1")):
            frees[l, "xkv", s] = n
        frees.update({(l, "wo", 3): "wo3", (l, "xq", 0): "xq0", (l, "xq", 1): "xq1", (l, "xo", 1): "xw3"})
    for half in range(2):
        frees.update({(0, "g", half, KT // 2 - 1): f"g{half}1{HB - 1}", (0, "u", half, KT // 2 - 1): f"u{half}1{HB - 1}",
                      (0, "d", half, HSLOT - 1): f"d{half}11"})
    fill_names = list(fill_at)
    used_count, slots_used_total = {}, 0
    split_names = [n for n in fill_names if n[1] not in ("wo", "xo")]
    split_at = {n: i for i, n in enumerate(split_names)}
    NSPLIT = len(split_names)
    for name in fill_names:
        if name not in frees:
            slots_used_total += 1
            used_count[name] = slots_used_total
    PASS_FILLS = 2 * KT + DSLOT
    assert PASS_FILLS % NSLOT == 0 and NSTATIC % NSLOT == 0 and NSPLIT % 2 == 0

    with ExitStack() as ctx:
        def sb(name, shape, dt=F32):
            return ctx.enter_context(nc.sbuf_tensor(name, shape, dt))

        def sem(name):
            return ctx.enter_context(nc.semaphore(name))

        ring = sb("ring", [P, NSLOT, SLOT])
        xres = sb("xres", [P, TT, D])
        with nc.sbuf_tensor("xn", [P, TT, D], F32) as xn:
            pass
        aT_low = sb("aT_low", [P, KT, S], F32R)
        with nc.sbuf_tensor("hT", [P, KT, S], F32) as hT:
            pass
        aT = sb("aT", [P, KT, S], F32R)
        memT = sb("memT", [P, KT, S])
        wh = sb("wh", [P, 2, SLOT], F32R)
        wl = sb("wl", [P, 2, SLOT], F32R)
        xk = sb("xk", [P, XH, S])
        xv = sb("xv", [P, 2, XH * XHD])
        with nc.sbuf_tensor("scratch", [P, 13 * 1024], F32) as scratch:
            pass
        ffn = sb("ffn", [P, 3584])
        xh = sb("xh", [P, KT, S], F32R)
        xl = sb("xl", [P, KT, S], F32R)
        ah = sb("ah", [P, DFF], F32R)
        al = sb("al", [P, DFF], F32R)
        psum = [ctx.enter_context(nc.psum_tensor(f"bank{b}", [P, BANK], F32)) for b in range(NBANK)]

        def part(at, *shape):
            n = int(np.prod(shape))
            ap = scratch[:, at:at + n]
            if len(shape) == 1:
                return ap
            names = "abc"[:len(shape)]
            return ap.rearrange(f"p ({' '.join(names)}) -> p {' '.join(names)}",
                                **{n_: s_ for n_, s_ in zip(names, shape)})

        zc = part(0, 12, S)
        zqk = part(3072, 8, S)
        sq = part(5120, 8, S)
        memraw = part(5120, TT, D)
        sc = part(5120, FH, 3 * P)
        osq = part(5120, TT * FH, HD)
        vtok = part(8192, 2, FH * HD)
        decay = part(9216, FH, 3 * P)
        pT = part(9216, FH, 3 * P)
        otok = part(12288, TT, FH * HD)
        ksq = part(12288, XH, S)
        mem_gained = xn[:].rearrange("p t (k s) -> p (t k) s", s=S)
        yT = xn[:].rearrange("p t (k s) -> p (t k) s", s=S)
        xsc = part(5120, XH, 2, S)
        xpT = part(9216, XH, 2, S)
        hid = ffn[:, 0:2 * HALF].rearrange("p (t f) -> p t f", t=TT)
        h1 = ffn[:, 0:DFF]
        yexp = ffn[:, 0:D]
        oneh = ffn[:, DFF:DFF + 256].rearrange("p (t s) -> p t s", t=TT)
        gated = ffn[:, DFF + 256:DFF + 512].rearrange("p (t s) -> p t s", t=TT)
        gatedT = ffn[:, DFF + 512:DFF + 768]

        ident = sb("ident", [P, P])
        tri8 = sb("tri8", [P, S])
        after = sb("after", [P, 3 * P])
        mask = sb("mask", [P, 3 * P])
        selg = sb("selg", [P, 30])
        selh = sb("selh", [P, 7])
        spreadg = sb("spreadg", [16, 8 * P])
        spreadh = sb("spreadh", [4, 4 * P])
        ones1 = sb("ones1", [1, P])
        neghalf = sb("neghalf", [P, 1])
        place = sb("place", [P, PASS_CAP])
        eight = sb("eight", [P, NE])
        NV = 56
        vrows = scratch[0:2 * NV, 0:P]
        vcols = sb("vcols", [P, 2 * NV])
        wf = part(P, L * KT, FH)
        wf_high = sb("wf_high", [P, L * KT, FH], F32R)
        wf_low = sb("wf_low", [P, L * KT, FH], F32R)
        wr = sb("wr", [P, KT, NE])
        brow = sb("brow", [1, L * FH + NE])
        msq = sb("msq", [P, 8])
        mqk = sb("mqk", [16, S])
        mcv = sb("mcv", [8, S])
        mmk = sb("mmk", [4, S])
        mxq = mmk
        newton = sb("newton", [16, S])
        epscol = sb("epscol", [16, 1])
        mfox = sb("mfox", [P, TT * FH])
        fz = sb("fz", [P, 4, TT * FH])
        negmax = sb("negmax", [P, 2, FH])
        denom = sb("denom", [P, 2, FH])
        xnm = sb("xnm", [P, XH, 2])
        xden = sb("xden", [P, XH, 2])
        top = sb("top", [P, TT, 8])
        topi = sb("topi", [P, TT, 8], U32)
        topf = sb("topf", [P, TT, 8])
        logit = sb("logit", [P, TT, NE])
        gw = sb("gw", [P, TT, 4])
        hot = sb("hot", [P, TT, 3, NE])
        gates = sb("gates", [P, TT, 2 * NE + 1])
        pos = sb("pos", [P, TT, 2 * NE + 1])
        cnt = sb("cnt", [1, 4])
        npass = sb("npass", [1, 1], I32)

        vec, nrow = {}, 0
        for nm, k in (("mix", 8), ("xa", 8), ("mem", 8), ("ffn", 8), ("tap", 12), ("cv", 4), ("fox", 4),
                      ("xq", 1), ("xk", 1), ("q", 1), ("k", 1)):
            for l in range(L):
                vec[l, nm] = nrow
                nrow += k
        assert nrow == 2 * NV

        def col(l, nm, i=0, n=1):
            return vcols[:, vec[l, nm] + i:vec[l, nm] + i + n]

        psum_full = [sem(f"psum_full{b}") for b in range(NBANK)]
        psum_taken = [sem(f"psum_taken{b}") for b in range(NBANK)]
        slot_filled = [sem(f"slot_filled{s}") for s in range(NSLOT)]
        slots_used = sem("slots_used")
        x_loaded = sem("x_loaded")
        mem_loaded = sem("mem_loaded")
        params_loaded = sem("params_loaded")
        pool_step = sem("pool_step")
        dve_step = sem("dve_step")
        act_step = sem("act_step")
        consts_ready = sem("consts_ready")
        ident_ready = sem("ident_ready")
        meansq_ready = sem("meansq_ready")
        rstd_ready = sem("rstd_ready")
        guess_ready = sem("guess_ready")
        rows_ready = sem("rows_ready")
        xn_ready = sem("xn_ready")
        fabs_ready = sem("fabs_ready")
        fln_ready = sem("fln_ready")
        logf_ready = sem("logf_ready")
        decay_ready = sem("decay_ready")
        squares_ready = sem("squares_ready")
        qk_ready = sem("qk_ready")
        memg_ready = sem("memg_ready")
        negmax_ready = sem("negmax_ready")
        probs_ready = sem("probs_ready")
        conv_ready = sem("conv_ready")
        osum_ready = sem("osum_ready")
        onorm_ready = sem("onorm_ready")
        xmax_ready = sem("xmax_ready")
        xprobs_ready = sem("xprobs_ready")
        xpn_ready = sem("xpn_ready")
        topd_ready = sem("topd_ready")
        tope_ready = sem("tope_ready")
        sel_ready = sem("sel_ready")
        route_ready = sem("route_ready")
        oneh_ready = sem("oneh_ready")
        gated_ready = sem("gated_ready")
        high_ready = sem("high_ready")
        low_ready = sem("low_ready")
        highs_used = sem("highs_used")
        wf_split = sem("wf_split")
        acthigh_ready = sem("acthigh_ready")
        stored = sem("stored")

        RSTDS = {}
        ROWS = {}
        SQUARES = {}
        for l in range(L):
            for n in ["mix"] + (["mem"] if l == 0 else []) + ["fox", "xa", "ffn"]:
                RSTDS[l, n] = len(RSTDS) + 1
            for n in ["qk0", "qk1", "qk2", "qk3", "mk", "cv", "fox", "xq"]:
                SQUARES[l, n] = len(SQUARES) + 1
            for n in ["qk", "cv", "mk", "xq"]:
                ROWS[l, n] = len(ROWS) + 1

        HIGHS = {}
        nhighs = 0
        for n, k in [((0, "xT"), 4), ((0, "yT"), 4), ((0, "zT"), 4), ((0, "hT0"), -(-HT // 2)), ((0, "hT1"), -(-HT // 2)),
                     ((1, "xT"), 4), ((1, "yT"), 4), ("passes", 0)]:
            HIGHS[n] = nhighs
            nhighs += k
        XN = {}
        for n in [(0, "mix"), (0, "mem"), (0, "xa"), (0, "ffn"), (1, "mix"), (1, "xa"), (1, "ffn")]:
            XN[n] = TT * (len(XN) + 1)
        NPARAMS = 18

        def bank(l, n):
            return psum[plan.at[l, n][0]]

        def full(l, n):
            b, use = plan.at[l, n]
            return psum_full[b], use + 1

        def taken(l, n):
            b, use = plan.at[l, n]
            return psum_taken[b], use + 1

        def take(l, n):
            return psum_taken[plan.at[l, n][0]]

        def lbank(n):
            return psum[in_pass.at[n][0]]

        def lcount(n, p):
            b, use = in_pass.at[n]
            return p * in_pass.uses[b] + (loop_base[b] + use)

        def lfull(n, p):
            return psum_full[in_pass.at[n][0]], lcount(n, p) + 1

        def ltaken(n, p):
            return psum_taken[in_pass.at[n][0]], lcount(n, p) + 1

        def ltake(n):
            return psum_taken[in_pass.at[n][0]]

        def pe_done_static(name):
            if name in frees:
                return full(name[0], frees[name])
            return slots_used, used_count[name]

        def pe_done_in_pass(j, p):
            if j < 0 and j + PASS_FILLS == PASS_FILLS - 1:
                return psum_full[in_pass.at["d1"][0]], lcount("d1", p) + (1 - in_pass.uses[in_pass.at["d1"][0]])
            ends = {KT - 1: f"g{FB - 1}", 2 * KT - 1: f"u{FB - 1}", PASS_FILLS - 1: "d1"}
            if j in ends:
                return lfull(ends[j], p)
            before = sum(1 for k in ends if k < j)
            return slots_used, p * (PASS_FILLS - 3) + (slots_used_total + j - before + 1)

        def fill_width(j):
            j = j % PASS_FILLS
            return DFF if j < 2 * KT else min(DROWS, FT - DROWS * (j - 2 * KT)) * D

        block = ctx.enter_context(nc.Block())

        @block.sync
        def _(sp):
            def slot_free(name):
                if name in split_at:
                    sp.wait_ge(low_ready, split_at[name] + 1)
                elif name in frees:
                    sp.wait_ge(*full(name[0], frees[name]))
                else:
                    sp.wait_ge(slots_used, used_count[name])

            def slot_free_in_pass(j, p):
                sp.wait_ge(low_ready, p * PASS_FILLS + (NSPLIT + j + 1))

            sp.dma_start(xres[:], x[0].rearrange("(t p) d -> p t d", p=P)).then_inc(x_loaded, 16)
            for n, (src, (k, c)) in enumerate(fills):
                if n >= NSLOT:
                    slot_free(fill_names[n - NSLOT])
                dst = ring[:, n % NSLOT, 0:k * c].rearrange("p (k c) -> p k c", k=k)
                sp.dma_start(dst, src).then_inc(slot_filled[n % NSLOT], 16)
                if n == 0:
                    for nm, src in (("mix", g_mix), ("xa", g_xa), ("mem", g_mem), ("ffn", g_ffn), ("cv", g_conv_out),
                                    ("fox", g_fox_out), ("xq", g_xq), ("xk", g_xk)):
                        r, k = vec[0, nm], L * src.shape[1] // P
                        sp.dma_start(vrows[r:r + k, :], src.rearrange("l (k p) -> (l k) p", p=P)).then_inc(params_loaded, 16)
                    r = vec[0, "tap"]
                    sp.dma_start(vrows[r:r + 12 * L, :], conv_w.rearrange("l j (k p) -> (l j k) p", p=P)).then_inc(params_loaded, 16)
                    for nm, src in (("q", g_q), ("k", g_k)):
                        r = vec[0, nm]
                        for half in range(2):
                            sp.dma_start(vrows[r:r + L, half * HD:half * HD + HD], src).then_inc(params_loaded, 16)
                    for l in range(L):
                        sp.dma_start(wf[:, KT * l:KT * l + KT], w_in[l][:, ICOLS - FH:ICOLS].rearrange("(k p) c -> p k c", p=P)).then_inc(params_loaded, 16)
                    sp.dma_start(brow[0:1, 0:L * FH], b_f.rearrange("l h -> (l h)").unsqueeze(0)).then_inc(params_loaded, 16)
                    sp.dma_start(wr[:], w_router[0].rearrange("(k p) c -> p k c", p=P)).then_inc(params_loaded, 16)
                    sp.dma_start(brow[0:1, L * FH:L * FH + NE], b_router[0:1, :]).then_inc(params_loaded, 16)
                    sp.dma_start(memraw, mem[0].rearrange("(t p) d -> p t d", p=P)).then_inc(mem_loaded, 16)

            wg_rows = we_gate[0].rearrange("e d f -> (e d) f")
            wu_rows = we_up[0].rearrange("e d f -> (e d) f")
            wd_rows = we_down[0].rearrange("e (k p) c -> p (e k) c", p=P)
            def load_expert(e, p, j):
                slot = (NSTATIC + j) % NSLOT
                if j < 2 * KT:
                    rows = wg_rows if j < KT else wu_rows
                    sp.dma_start(ring[:, slot, 0:DFF], rows[bass.ds(e * D + (j % KT) * P, P), :]
                                 ).then_inc(slot_filled[slot], 16)
                else:
                    k0 = (j - 2 * KT) * DROWS
                    k = min(DROWS, FT - k0)
                    dst = ring[:, slot, 0:k * D].rearrange("p (k c) -> p k c", k=k)
                    sp.dma_start(dst, wd_rows[:, bass.ds(e * FT + k0, k), :]).then_inc(slot_filled[slot], 16)

            for j in range(NSLOT):
                slot_free(fill_names[NSTATIC - NSLOT + j])
                load_expert(0, 0, j)
            sp.wait_ge(route_ready, 1)
            rounds = sp.value_load(npass[0:1, 0:1], min_val=1, max_val=2)
            with sp.Fori(0, rounds) as rnd:
                with sp.Fori(0, NE) as e:
                    p = rnd * NE + e
                    for j in range(NSLOT, PASS_FILLS):
                        slot_free_in_pass(j - NSLOT, p)
                        load_expert(e, p, j)
                    for j in range(NSLOT):
                        slot_free_in_pass(j + PASS_FILLS - NSLOT, p)
                        load_expert((e + 1) % NE, p, j)
            for i in range(4):
                sp.wait_ge(*ltaken(f"sc{i}", rounds * NE - 1))
            for s in range(NSLOT):
                sp.wait_ge(slot_filled[s], rounds * (16 * NE * (PASS_FILLS // NSLOT)) + 16 * (NSTATIC // NSLOT + 1))
            sp.dma_start(out[0].rearrange("(t p) d -> p t d", p=P), xres[:]).then_inc(stored, 16)
            sp.wait_ge(stored, 16)

        @block.gpsimd
        def _(pool):
            steps = [0]

            def then_wait(ins):
                steps[0] += 1
                ins.then_inc(pool_step, 1)
                pool.wait_ge(pool_step, steps[0])

            def select(ap, pattern, op, fill, base, mult):
                return nc.gpsimd.affine_select(out=ap, in_=ap, pattern=pattern, compare_op=op, fill=fill,
                                               base=base, channel_multiplier=mult)

            then_wait(nc.gpsimd.memset(ident[:], 0.0))
            select(ident[:], [[-1, P]], ALU.not_equal, 1.0, 0, 1).then_inc(ident_ready, 1)
            nc.gpsimd.memset(ones1[:], 1.0)
            nc.gpsimd.memset(neghalf[:], -0.5)
            nc.gpsimd.memset(epscol[:], EPS)
            nc.gpsimd.memset(tri8[:], 8.0)
            nc.gpsimd.memset(after[:], 1.0)
            nc.gpsimd.memset(mask[:], 0.0)
            nc.gpsimd.memset(selg[:], 0.0)
            nc.gpsimd.memset(selh[:], 0.0)
            nc.gpsimd.memset(spreadg[:], 1.0)
            then_wait(nc.gpsimd.memset(spreadh[:], 1.0))
            nc.gpsimd.memset(selh[:, 3:4], 1.0 / XHD)
            then_wait(nc.gpsimd.memset(selg[:, 14:16], 1.0 / HD))
            select(selg[:, 14:15], [[0, 1]], ALU.is_ge, 0.0, HD - 1, -1)
            select(selg[:, 15:16], [[0, 1]], ALU.is_ge, 0.0, -HD, 1)
            select(tri8[:], [[1, S]], ALU.is_ge, 0.0, 0, -1)
            for c in (0, 2 * P):
                select(after[:, c:c + P], [[-1, P]], ALU.is_gt, 0.0, 0, 1)
                select(mask[:, c:c + P], [[-1, P]], ALU.is_ge, MASKED, 0, 1)
            select(spreadg[:], [[1, 8 * P]], ALU.is_ge, 0.0, 0, -HD)
            then_wait(select(spreadh[:], [[1, 4 * P]], ALU.is_ge, 0.0, 0, -XHD))
            select(spreadg[:], [[-1, 8 * P]], ALU.is_ge, 0.0, HD - 1, HD)
            then_wait(select(spreadh[:], [[-1, 4 * P]], ALU.is_ge, 0.0, XHD - 1, XHD))
            nc.gpsimd.iota(place[:], [[1, PASS_CAP]], base=0, channel_multiplier=0,
                           allow_small_or_imprecise_dtypes=True)
            nc.gpsimd.iota(eight[:], [[1, NE]], base=0, channel_multiplier=0,
                           allow_small_or_imprecise_dtypes=True).then_inc(consts_ready, 1)

            def rstd(ap):
                then_wait(nc.gpsimd.tensor_scalar(ap, ap, EPS, None, ALU.add))
                rows, n = ap.shape
                nc.gpsimd.tensor_tensor(ap, ap, neghalf[0:rows, :].to_broadcast([rows, n]), ALU.pow).then_inc(rstd_ready, 1)

            norms = 0
            for l in range(L):
                norms += TT
                pool.wait_ge(meansq_ready, norms)
                rstd(msq[:, 0:2])
                if l == 0:
                    norms += TT
                    pool.wait_ge(meansq_ready, norms)
                    rstd(msq[:, 2:4])
                pool.wait_ge(logf_ready, l + 1)
                nc.gpsimd.tensor_tensor(
                    decay[:, :, 0:S], tri8[:].unsqueeze(1).to_broadcast([P, FH, S]),
                    bcast_last(fz[:, 3, 0:FH], S), ALU.mult)
                nc.gpsimd.tensor_tensor(
                    decay[:, :, S:3 * P], tri8[:, 0:P].unsqueeze(1).to_broadcast([P, FH, P]),
                    bcast_last(fz[:, 3, FH:2 * FH], P), ALU.mult).then_inc(decay_ready, 1)
                pool.wait_ge(*full(l, "conv5"))
                if l == 0:
                    pool.wait_ge(*taken(0, "vec"))
                    for i in range(4):
                        pool.wait_ge(*taken(0, f"mT{i}"))
                then_wait(nc.gpsimd.tensor_tensor(mem_gained, memT[:], bcast_last(col(l, "mem", 0, KT), S), ALU.mult))
                then_wait(nc.gpsimd.tensor_copy(aT[:], mem_gained))
                nc.gpsimd.tensor_tensor(aT_low[:], mem_gained, aT[:].bitcast(F32), ALU.subtract).then_inc(memg_ready, 1)
                pool.wait_ge(osum_ready, l + 1)
                rstd(mfox[:])
                norms += TT
                pool.wait_ge(meansq_ready, norms)
                rstd(msq[:, 0:2])
                norms += TT
                pool.wait_ge(meansq_ready, norms)
                rstd(msq[:, 0:2])

        @block.scalar
        def _(act):
            steps = [0]

            def then_wait(ins):
                steps[0] += 1
                ins.then_inc(act_step, 1)
                act.wait_ge(act_step, steps[0])

            def square(l, n, dst, src, scale=1.0):
                nc.scalar.activation(dst, src, ACT.Square, scale=scale).then_inc(squares_ready, 1)

            def mean_squares(l, added):
                for t in range(TT):
                    for n in added[2 * t:2 * t + 2]:
                        if n[0] != "d":
                            act.wait_ge(*taken(l, n))
                        elif l == 1:
                            act.wait_ge(*taken(0, n))
                    nc.scalar.activation(xn[:, t, :], xres[:, t, :], ACT.Square, scale=D ** -0.5,
                                         accum_out=msq[:, t:t + 1]).then_inc(meansq_ready, 1)

            def guess_rows(l, n, result, dst):
                rows = dst.shape[0]
                act.wait_ge(*full(l, result))
                then_wait(nc.scalar.activation(dst, bank(l, result)[0:rows, 0:S], ACT.Ln, bias=epscol[0:rows, :]))
                nc.scalar.activation(dst, dst, ACT.Exp, scale=-0.5).then_inc(guess_ready, 1)

            def high(slot, n, j):
                nc.scalar.activation(wh[:, j, 0:n], ring[:, slot, 0:n], ACT.Copy).then_inc(high_ready, 1)

            def high_static(i):
                n = fill_at[split_names[i]]
                act.wait_ge(slot_filled[n % NSLOT], 16 * (n // NSLOT + 1))
                if i >= 2:
                    act.wait_ge(highs_used, i - 1)
                high(n % NSLOT, int(np.prod(fills[n][1])), i % 2)

            def high_in_pass(j, p):
                slot = j % NSLOT
                act.wait_ge(slot_filled[slot], p * (16 * (PASS_FILLS // NSLOT)) + 16 * ((NSTATIC + j) // NSLOT + 1))
                act.wait_ge(highs_used, p * PASS_FILLS + (NSPLIT + j - 1))
                high(slot, fill_width(j), j % 2)

            def gained(l, names, gain):
                for i in (1, 3):
                    act.wait_ge(*full(l, f"{names}{i}"))
                    for k in range(2):
                        c = 2 * i + k
                        ins = nc.scalar.activation(hT[:, c, :], bank(l, f"{names}{i}")[:, k * S:k * S + S], ACT.Copy,
                                                   scale=col(l, gain, c))
                    ins.then_inc(take(l, f"{names}{i}"), 1)

            def input_high(l, names, gain):
                for i in range(4):
                    act.wait_ge(*full(l, f"{names}{i}"))
                    for k in range(2):
                        c = 2 * i + k
                        ins = nc.scalar.activation(aT[:, c, :], bank(l, f"{names}{i}")[:, k * S:k * S + S], ACT.Copy,
                                                   scale=col(l, gain, c))
                    ins.then_inc(acthigh_ready, 1)

            def high_of(l, name, *which):
                for s in which:
                    high_static(split_at[l, name, s])

            for l in range(L):
                if l == 0:
                    act.wait_ge(x_loaded, 16)
                else:
                    high_of(l, "z", 0, 1)
                mean_squares(l, ["d100", "d101", "d110", "d111"])
                if l == 0:
                    act.wait_ge(params_loaded, 16 * NPARAMS)
                    nc.scalar.activation(wf_high[:], wf, ACT.Copy).then_inc(wf_split, 1)
                    high_of(0, "z", 0)
                    act.wait_ge(*taken(0, "vec"))
                input_high(l, "xT", "mix")
                if l == 0:
                    act.wait_ge(mem_loaded, 16)
                    for t in range(TT):
                        nc.scalar.activation(memT[:].rearrange("p k s -> p (k s)")[:, t * D:t * D + D], memraw[:, t, :],
                                             ACT.Square, scale=D ** -0.5,
                                             accum_out=msq[:, 2 + t:3 + t]).then_inc(meansq_ready, 1)
                    high_of(0, "z", 1)
                act.wait_ge(fabs_ready, l + 1)
                then_wait(nc.scalar.activation(fz[:, 2, :], fz[:, 1, :], ACT.Exp))
                nc.scalar.activation(fz[:, 2, :], fz[:, 2, :], ACT.Ln, bias=1.0).then_inc(fln_ready, 1)
                for i in range(4):
                    act.wait_ge(*taken(l, f"qk{i}"))
                    square(l, f"qk{i}", sq[:, 2 * i:2 * i + 2, :], zqk[:, 2 * i:2 * i + 2, :])
                    if i in (0, 2):
                        high_of(l, "z", 2 + i // 2)
                high_of(l, "z", 4)
                for i in range(2):
                    act.wait_ge(*full(l, f"v{i}"))
                    nc.scalar.activation(vtok[:, i, :], bank(l, f"v{i}")[:], ACT.Copy).then_inc(take(l, f"v{i}"), 1)
                high_of(l, "z", 5)
                guess_rows(l, "qk", "ssqk", mqk[:])
                for i in range(4):
                    act.wait_ge(*full(l, f"conv{i}"))
                    nc.scalar.activation(zc[:, 2 * i:2 * i + 2, :].rearrange("p a s -> p (a s)"), bank(l, f"conv{i}")[:],
                                         ACT.Copy).then_inc(take(l, f"conv{i}"), 1)
                    if i in (0, 2):
                        high_of(l, "z", 6 + i // 2)
                high_of(l, "xkv", 0, 1)
                for h in range(FH):
                    act.wait_ge(negmax_ready, 4 * l + 2 * (h // 4 + 1))
                    for q, (a, b) in enumerate(((0, P), (P, 3 * P))):
                        nc.scalar.activation(sc[:, h, a:b], sc[:, h, a:b], ACT.Exp, bias=negmax[:, q, h:h + 1],
                                             accum_out=denom[:, q, h:h + 1]).then_inc(probs_ready, 1)
                    if h % 4 == 3:
                        high_of(l, "xkv", 2 + h // 4)
                for i in range(2):
                    act.wait_ge(*full(l, f"mk{i}"))
                    nc.scalar.activation(xk[:, 2 * i:2 * i + 2, :].rearrange("p a s -> p (a s)"), bank(l, f"mk{i}")[:],
                                         ACT.Copy).then_inc(take(l, f"mk{i}"), 1)
                for i in range(2):
                    act.wait_ge(*taken(l, f"mk{i}"))
                square(l, "mk", ksq, xk[:])
                for i in range(2):
                    act.wait_ge(*full(l, f"mv{i}"))
                    nc.scalar.activation(xv[:, i, :], bank(l, f"mv{i}")[:], ACT.Copy).then_inc(take(l, f"mv{i}"), 1)
                act.wait_ge(conv_ready, l + 1)
                square(l, "cv", zc[:, 4:8, :], zc[:, 0:4, :])
                guess_rows(l, "cv", "ssc", mcv[:])
                guess_rows(l, "mk", "ssmk", mmk[:])
                for h in range(1, FH, 2):
                    act.wait_ge(*full(l, f"pt{h}"))
                    nc.scalar.activation(pT[:, h, :], bank(l, f"pt{h}")[:, 0:3 * P], ACT.Copy).then_inc(take(l, f"pt{h}"), 1)
                for i in range(2):
                    act.wait_ge(*taken(l, f"o{i}"))
                square(l, "fox", osq.rearrange("p a b -> p (a b)"), otok.rearrange("p a b -> p (a b)"), scale=HD ** -0.5)

                high_of(l, "xq", 0, 1)
                mean_squares(l, [f"wo{i}" for i in range(4)])
                input_high(l, "yT", "xa")
                for i in range(2):
                    act.wait_ge(*taken(l, f"xq{i}"))
                square(l, "xq", sq[:, 0:4, :], zqk[:, 0:4, :])
                guess_rows(l, "xq", "ssxq", mxq[:])
                for h in range(XH):
                    act.wait_ge(xmax_ready, XH * l + h + 1)
                    for q in range(2):
                        ins = nc.scalar.activation(xsc[:, h, q, :], bank(l, f"xs{h}")[:, q * S:q * S + S], ACT.Exp,
                                                   bias=xnm[:, h, q:q + 1], scale=XHD ** -0.5,
                                                   accum_out=xden[:, h, q:q + 1])
                        if q == 0:
                            ins.then_inc(xprobs_ready, 1)
                    ins.then_inc(take(l, f"xs{h}"), 1)
                for h in range(1, XH, 2):
                    act.wait_ge(*full(l, f"xpt{h}"))
                    nc.scalar.activation(xpT[:, h].rearrange("p a s -> p (a s)"), bank(l, f"xpt{h}")[:],
                                         ACT.Copy).then_inc(take(l, f"xpt{h}"), 1)
                for i in range(2):
                    act.wait_ge(*full(l, f"xo{i}"))
                    nc.scalar.activation(zqk[:, 4 + 2 * i:6 + 2 * i, :].rearrange("p a s -> p (a s)"),
                                         bank(l, f"xo{i}")[:], ACT.Copy).then_inc(take(l, f"xo{i}"), 1)

                mean_squares(l, [f"xw{i}" for i in range(4)])
                if l > 0:
                    gained(l, "zT", "ffn")
                if l == 0:
                    for i in range(4):
                        act.wait_ge(*full(0, f"zT{i}"))
                        for k in range(2):
                            c = 2 * i + k
                            ins = nc.scalar.activation(xh[:, c, :], bank(0, f"zT{i}")[:, k * S:k * S + S], ACT.Copy,
                                                       scale=col(0, "ffn", c))
                        ins.then_inc(acthigh_ready, 1)
                    for half in range(2):
                        base = split_at[0, "g", half, 0]
                        for i in range(half, 5):
                            high_static(base + i)
                        for t in range(TT):
                            for i in range(HB):
                                a, b = i * BANK, min(i * BANK + BANK, HALF)
                                act.wait_ge(*full(0, f"g{half}{t}{i}"))
                                nc.scalar.activation(hid[:, t, a:b], bank(0, f"g{half}{t}{i}")[:, 0:b - a],
                                                     ACT.Silu).then_inc(take(0, f"g{half}{t}{i}"), 1)
                        for i in range(5, 9):
                            high_static(base + i)
                        for i in range(-(-HT // 2)):
                            k = min(2, HT - 2 * i)
                            act.wait_ge(*full(0, f"hT{half}{i}"))
                            nc.scalar.activation(ah[:, i * BANK:i * BANK + k * S], bank(0, f"hT{half}{i}")[:, 0:k * S],
                                                 ACT.Copy).then_inc(acthigh_ready, 1)
                        for i in range(9, 13 if half == 0 else 12):
                            high_static(base + i)
                else:
                    act.wait_ge(topd_ready, 1)
                    nc.scalar.activation(gw[:, :, 1:2], gw[:, :, 0:1], ACT.Exp).then_inc(tope_ready, 1)

            def gathered_high(wait):
                for i in range(2):
                    act.wait_ge(*wait(f"ga{i}")[0])
                    for k in range(4):
                        c = 4 * i + k
                        ins = nc.scalar.activation(xh[:, c, 0:PASS_CAP], wait(f"ga{i}")[1][:, k * P:k * P + P], ACT.Copy,
                                                   scale=col(L - 1, "ffn", c))
                    ins.then_inc(acthigh_ready, 1)

            high_in_pass(0, 0)
            gathered_high(lambda n: (full(L - 1, n), bank(L - 1, n)))

            act.wait_ge(route_ready, 1)
            rounds = act.value_load(npass[0:1, 0:1], min_val=1, max_val=2)
            with act.Fori(0, rounds) as rnd:
                with act.Fori(0, NE) as e:
                    p = rnd * NE + e

                    for j in range(1, KT + 1):
                        high_in_pass(j, p)
                    for i in range(FB):
                        a, b = i * BANK, min(i * BANK + BANK, DFF)
                        act.wait_ge(*lfull(f"g{i}", p))
                        nc.scalar.activation(h1[:, a:b], lbank(f"g{i}")[:, 0:b - a], ACT.Silu).then_inc(ltake(f"g{i}"), 1)
                    for j in range(KT + 1, 2 * KT + 2):
                        high_in_pass(j, p)
                    for i in range(FB):
                        k = min(4, FT - 4 * i)
                        act.wait_ge(*lfull(f"hT{i}", p))
                        nc.scalar.activation(ah[:, i * BANK:i * BANK + k * P], lbank(f"hT{i}")[:, 0:k * P],
                                             ACT.Copy).then_inc(acthigh_ready, 1)
                    high_in_pass(2 * KT + 2, p)
                    gathered_high(lambda n: (lfull(n, p), lbank(n)))
                    for j in range(2 * KT + 3, PASS_FILLS):
                        high_in_pass(j, p)
                    high_in_pass(PASS_FILLS, p)
                    for i in range(2):
                        act.wait_ge(*lfull(f"d{i}", p))
                        nc.scalar.activation(yexp[:, i * BANK:i * BANK + BANK], lbank(f"d{i}")[:],
                                             ACT.Copy).then_inc(ltake(f"d{i}"), 1)

        @block.vector
        def _(dve):
            steps = [0]

            def then_wait(ins):
                steps[0] += 1
                ins.then_inc(dve_step, 1)
                dve.wait_ge(dve_step, steps[0])

            def normalise(l, n, src, at, dst):
                dve.wait_ge(rstd_ready, RSTDS[l, n])
                for t in range(TT):
                    nc.vector.tensor_scalar(dst[:, t, :], src[:, t, :], msq[:, at + t:at + t + 1], None,
                                            ALU.mult).then_inc(xn_ready, 1)

            def refine_rows(l, n, result, y):
                rows = y.shape[0]
                u = newton[0:rows, :]
                if ROWS[l, n] > 1:
                    dve.wait_ge(rows_ready, ROWS[l, n] - 1)
                dve.wait_ge(guess_ready, ROWS[l, n])
                then_wait(nc.vector.tensor_tensor(u, y, y, ALU.mult))
                nc.vector.scalar_tensor_tensor(u, bank(l, result)[0:rows, 0:S], EPS, u, ALU.add, ALU.mult
                                               ).then_inc(take(l, result), 1)
                dve.wait_ge(*taken(l, result))
                then_wait(nc.vector.tensor_scalar(u, u, -0.5, 1.5, ALU.mult, ALU.add))
                nc.vector.tensor_tensor(y, y, u, ALU.mult).then_inc(rows_ready, 1)

            def low(slot, n, j):
                nc.vector.tensor_tensor(wl[:, j, 0:n], ring[:, slot, 0:n], wh[:, j, 0:n].bitcast(F32), ALU.subtract
                                        ).then_inc(low_ready, 1)

            def low_static(i):
                n = fill_at[split_names[i]]
                dve.wait_ge(high_ready, i + 1)
                if i >= 2:
                    dve.wait_ge(*pe_done_static(split_names[i - 2]))
                low(n % NSLOT, int(np.prod(fills[n][1])), i % 2)

            def low_in_pass(j, p):
                dve.wait_ge(high_ready, p * PASS_FILLS + (NSPLIT + j + 1))
                dve.wait_ge(*pe_done_in_pass(j - 2, p))
                low(j % NSLOT, fill_width(j), j % 2)

            def act_low(dst, src, high_, gain=None):
                if gain is None:
                    return nc.vector.tensor_tensor(dst, src, high_.bitcast(F32), ALU.subtract)
                return nc.vector.scalar_tensor_tensor(dst, src, gain, high_.bitcast(F32), ALU.mult, ALU.subtract)

            def gained(l, names, gain):
                for i in (0, 2):
                    dve.wait_ge(*full(l, f"{names}{i}"))
                    nc.vector.tensor_tensor(hT[:, 2 * i:2 * i + 2, :], bank(l, f"{names}{i}")[:].rearrange("p (k s) -> p k s", k=2),
                                            bcast_last(col(l, gain, 2 * i, 2), S), ALU.mult).then_inc(take(l, f"{names}{i}"), 1)

            def add_residual(l, names):
                for t in range(TT):
                    for i in range(2):
                        n = f"{names}{2 * t + i}"
                        dve.wait_ge(*full(l, n))
                        xs = xres[:, t, i * BANK:i * BANK + BANK]
                        nc.vector.tensor_tensor(xs, xs, bank(l, n)[:], ALU.add).then_inc(take(l, n), 1)

            def input_low(l, names, gain):
                dve.wait_ge(*full(l, f"{names}3"))
                for i in range(4):
                    dve.wait_ge(acthigh_ready, HIGHS[l, names] + i + 1)
                    for k in range(2):
                        c = 2 * i + k
                        ins = act_low(aT_low[:, c, :], bank(l, f"{names}{i}")[:, k * S:k * S + S], aT[:, c, :], col(l, gain, c))
                    ins.then_inc(take(l, f"{names}{i}"), 1)

            def low_of(l, name, *which):
                for s in which:
                    low_static(split_at[l, name, s])

            for l in range(L):
                if l == 0:
                    dve.wait_ge(*full(0, "vec"))
                    nc.vector.tensor_copy(vcols[:], bank(0, "vec")[:, 0:2 * NV]).then_inc(take(0, "vec"), 1)
                else:
                    low_of(l, "z", 0)
                normalise(l, "mix", xres, 0, xn)
                if l == 0:
                    dve.wait_ge(wf_split, 1)
                    nc.vector.tensor_tensor(wf_low[:], wf, wf_high[:].bitcast(F32), ALU.subtract).then_inc(wf_split, 1)
                    dve.wait_ge(*taken(0, "vec"))
                input_low(l, "xT", "mix")
                if l == 0:
                    normalise(l, "mem", memraw, 2, memraw)
                    low_of(0, "z", 0)
                low_of(l, "z", 1)
                dve.wait_ge(*full(l, "f"))
                nc.vector.tensor_copy(fz[:, 0, :], bank(l, "f")[:, 0:TT * FH]).then_inc(take(l, "f"), 1)
                dve.wait_ge(*taken(l, "f"))
                then_wait(nc.vector.tensor_scalar(fz[:, 3, :], fz[:, 0, :], 0.0, None, ALU.min))
                nc.vector.scalar_tensor_tensor(fz[:, 1, :], fz[:, 3, :], 2.0, fz[:, 0, :], ALU.mult, ALU.subtract
                                               ).then_inc(fabs_ready, 1)
                dve.wait_ge(fln_ready, l + 1)
                nc.vector.tensor_tensor(fz[:, 3, :], fz[:, 3, :], fz[:, 2, :], ALU.subtract).then_inc(logf_ready, 1)
                if l == 0:
                    for i in range(4):
                        dve.wait_ge(*full(l, f"mT{i}"))
                        nc.vector.tensor_copy(memT[:, 2 * i:2 * i + 2, :].rearrange("p k s -> p (k s)"), bank(l, f"mT{i}")[:]
                                              ).then_inc(take(l, f"mT{i}"), 1)
                for i in range(4):
                    dve.wait_ge(*full(l, f"qk{i}"))
                    nc.vector.tensor_copy(zqk[:, 2 * i:2 * i + 2, :].rearrange("p a s -> p (a s)"), bank(l, f"qk{i}")[:]
                                          ).then_inc(take(l, f"qk{i}"), 1)
                    if i in (1, 2):
                        low_of(l, "z", 1 + i)
                low_of(l, "z", 4, 5)
                refine_rows(l, "qk", "ssqk", mqk[:])
                low_of(l, "z", 6, 7)
                for i in range(2):
                    dve.wait_ge(*full(l, f"conv{4 + i}"))
                    dve.wait_ge(*taken(l, f"conv{2 + i}"))
                    u = zc[:, 4 + 2 * i:6 + 2 * i, :].rearrange("p a s -> p (a s)")
                    nc.vector.tensor_tensor(u, bank(l, f"conv{4 + i}")[:], u, ALU.mult).then_inc(take(l, f"conv{4 + i}"), 1)
                for i in range(4):
                    dve.wait_ge(*full(l, f"bq{i}"))
                    qk = zqk[:, 2 * i:2 * i + 2, :].rearrange("p a s -> p (a s)")
                    nc.vector.scalar_tensor_tensor(qk, qk, col(l, "q" if i < 2 else "k"), bank(l, f"bq{i}")[:],
                                                   ALU.mult, ALU.mult).then_inc(take(l, f"bq{i}"), 1)
                low_of(l, "xkv", 0)
                for h in range(FH):
                    dve.wait_ge(*full(l, f"s{h}"))
                    nc.vector.scalar_tensor_tensor(sc[:, h, :], bank(l, f"s{h}")[:, 0:3 * P], HD ** -0.5, mask[:],
                                                   ALU.mult, ALU.add).then_inc(take(l, f"s{h}"), 1)
                    if h % 4 == 3:
                        for i in range(4):
                            dve.wait_ge(*taken(l, f"s{h - i}"))
                        for q, (a, b) in enumerate(((0, P), (P, 3 * P))):
                            nc.vector.tensor_reduce(negmax[:, q, h - 3:h + 1], sc[:, h - 3:h + 1, a:b], AX_X, ALU.max,
                                                    negate=True).then_inc(negmax_ready, 1)
                        low_of(l, "xkv", 1 + h // 4)
                for i in range(2):
                    dve.wait_ge(*taken(l, f"conv{4 + i}"))
                    dve.wait_ge(*taken(l, f"conv{i}"))
                for j in range(4):
                    u, acc, bj = zc[:, 4 + j, :], zc[:, 8 + j, :], zc[:, j, :]
                    then_wait(nc.vector.tensor_scalar(acc, u, col(l, "tap", 8 + j), None, ALU.mult))
                    for back in (1, 2):
                        then_wait(nc.vector.scalar_tensor_tensor(acc[:, back:S], u[:, 0:S - back], col(l, "tap", 8 - 4 * back + j),
                                                                 acc[:, back:S], ALU.mult, ALU.add))
                    ins = nc.vector.tensor_tensor(bj, bj, acc, ALU.mult)
                    if j == 3:
                        ins.then_inc(conv_ready, 1)
                    else:
                        then_wait(ins)
                low_of(l, "xkv", 3)
                refine_rows(l, "cv", "ssc", mcv[:])
                refine_rows(l, "mk", "ssmk", mmk[:])

                def probs_out(*heads):
                    for h in heads:
                        dve.wait_ge(*full(l, f"pt{h}"))
                        nc.vector.tensor_copy(pT[:, h, :], bank(l, f"pt{h}")[:, 0:3 * P]).then_inc(take(l, f"pt{h}"), 1)

                probs_out(0, 2)
                dve.wait_ge(conv_ready, l + 1)
                for i in range(2):
                    dve.wait_ge(*full(l, f"bc{i}"))
                    for j in (2 * i, 2 * i + 1):
                        ins = nc.vector.scalar_tensor_tensor(yT[:, j, :], zc[:, j, :], col(l, "cv", j),
                                                             bank(l, f"bc{i}")[:, (j % 2) * S:(j % 2) * S + S], ALU.mult, ALU.mult)
                    ins.then_inc(take(l, f"bc{i}"), 1)
                for i in range(2):
                    dve.wait_ge(*full(l, f"bmk{i}"))
                    kk = xk[:, 2 * i:2 * i + 2, :].rearrange("p a s -> p (a s)")
                    nc.vector.scalar_tensor_tensor(kk, kk, col(l, "xk"), bank(l, f"bmk{i}")[:], ALU.mult, ALU.mult
                                                   ).then_inc(take(l, f"bmk{i}"), 1)
                dve.wait_ge(probs_ready, 16 * (l + 1))
                then_wait(nc.vector.reciprocal(denom[:], denom[:]))
                probs_out(4, 6)
                for q in range(2):
                    dve.wait_ge(*full(l, f"o{q}"))
                    nc.vector.tensor_tensor(otok[:, q, :].rearrange("p (h d) -> p h d", h=FH),
                                            bank(l, f"o{q}")[:].rearrange("p (h d) -> p h d", h=FH),
                                            bcast_last(denom[:, q, :], HD), ALU.mult).then_inc(take(l, f"o{q}"), 1)
                dve.wait_ge(squares_ready, SQUARES[l, "fox"])
                nc.vector.tensor_reduce(mfox[:], osq, AX_X, ALU.add).then_inc(osum_ready, 1)
                dve.wait_ge(rstd_ready, RSTDS[l, "fox"])
                ot = otok.rearrange("p t (h d) -> p (t h) d", d=HD)
                nc.vector.tensor_tensor(ot, ot, bcast_last(mfox[:], HD), ALU.mult).then_inc(onorm_ready, 1)
                for i in range(2):
                    dve.wait_ge(*full(l, f"oT{i}"))
                    nc.vector.tensor_tensor(yT[:, 4 + 2 * i:6 + 2 * i, :], bank(l, f"oT{i}")[:].rearrange("p (k s) -> p k s", k=2),
                                            bcast_last(col(l, "fox", 2 * i, 2), S), ALU.mult).then_inc(take(l, f"oT{i}"), 1)
                low_of(l, "xq", 0, 1)
                add_residual(l, "wo")

                normalise(l, "xa", xres, 0, xn)
                input_low(l, "yT", "xa")
                for i in range(2):
                    dve.wait_ge(*full(l, f"xq{i}"))
                    nc.vector.tensor_copy(zqk[:, 2 * i:2 * i + 2, :].rearrange("p a s -> p (a s)"), bank(l, f"xq{i}")[:]
                                          ).then_inc(take(l, f"xq{i}"), 1)
                refine_rows(l, "xq", "ssxq", mxq[:])
                for i in range(2):
                    dve.wait_ge(*full(l, f"bxq{i}"))
                    qq = zqk[:, 2 * i:2 * i + 2, :].rearrange("p a s -> p (a s)")
                    nc.vector.scalar_tensor_tensor(qq, qq, col(l, "xq"), bank(l, f"bxq{i}")[:], ALU.mult, ALU.mult
                                                   ).then_inc(take(l, f"bxq{i}"), 1)
                for h in range(XH):
                    dve.wait_ge(*full(l, f"xs{h}"))
                    then_wait(nc.vector.tensor_reduce(xnm[:, h, :], bank(l, f"xs{h}")[:].rearrange("p (q m) -> p q m", q=2),
                                                      AX_X, ALU.max, negate=True))
                    nc.vector.tensor_scalar(xnm[:, h, :], xnm[:, h, :], XHD ** -0.5, None, ALU.mult).then_inc(xmax_ready, 1)
                for h in range(XH):
                    dve.wait_ge(*taken(l, f"xs{h}"))
                    dve.wait_ge(xprobs_ready, XH * l + h + 1)
                    then_wait(nc.vector.reciprocal(xden[:, h, :], xden[:, h, :]))
                    nc.vector.tensor_tensor(xsc[:, h], xsc[:, h], bcast_last(xden[:, h, :], S), ALU.mult).then_inc(xpn_ready, 1)
                for h in range(0, XH, 2):
                    dve.wait_ge(*full(l, f"xpt{h}"))
                    nc.vector.tensor_copy(xpT[:, h].rearrange("p a s -> p (a s)"), bank(l, f"xpt{h}")[:]
                                          ).then_inc(take(l, f"xpt{h}"), 1)
                add_residual(l, "xw")

                normalise(l, "ffn", xres, 0, xn)
                if l > 0:
                    gained(l, "zT", "ffn")
                else:
                    for i in range(4):
                        dve.wait_ge(acthigh_ready, HIGHS[0, "zT"] + i + 1)
                        for k in range(2):
                            c = 2 * i + k
                            ins = act_low(xl[:, c, :], bank(0, f"zT{i}")[:, k * S:k * S + S], xh[:, c, :], col(0, "ffn", c))
                        ins.then_inc(take(0, f"zT{i}"), 1)
                    for half in range(2):
                        base = split_at[0, "g", half, 0]
                        for i in range(half, 8):
                            low_static(base + i)
                        for t in range(TT):
                            for i in range(HB):
                                a, b = i * BANK, min(i * BANK + BANK, HALF)
                                dve.wait_ge(*full(0, f"u{half}{t}{i}"))
                                dve.wait_ge(*taken(0, f"g{half}{t}{i}"))
                                nc.vector.tensor_tensor(hid[:, t, a:b], bank(0, f"u{half}{t}{i}")[:, 0:b - a], hid[:, t, a:b],
                                                        ALU.mult).then_inc(take(0, f"u{half}{t}{i}"), 1)
                        low_static(base + 8)
                        nT = -(-HT // 2)
                        for i in range(nT):
                            k = min(2, HT - 2 * i)
                            dve.wait_ge(acthigh_ready, HIGHS[0, f"hT{half}"] + i + 1)
                            act_low(al[:, i * BANK:i * BANK + k * S], bank(0, f"hT{half}{i}")[:, 0:k * S],
                                    ah[:, i * BANK:i * BANK + k * S]).then_inc(take(0, f"hT{half}{i}"), 1)
                        for i in range(9, 13 if half == 0 else 12):
                            low_static(base + i)
                        for t in range(TT):
                            for i in range(2):
                                dve.wait_ge(*full(0, f"d{half}{t}{i}"))
                                xs = xres[:, t, i * BANK:i * BANK + BANK]
                                nc.vector.tensor_tensor(xs, xs, bank(0, f"d{half}{t}{i}")[:], ALU.add
                                                        ).then_inc(take(0, f"d{half}{t}{i}"), 1)

            l = L - 1
            dve.wait_ge(*full(l, "r"))
            nc.vector.tensor_copy(logit[:].rearrange("p t e -> p (t e)"), bank(l, "r")[:, 0:TT * NE]).then_inc(take(l, "r"), 1)
            dve.wait_ge(*taken(l, "r"))
            for t in range(TT):
                then_wait(nc.vector.max(top[:, t, :], logit[:, t, :]))
                then_wait(nc.vector.max_index(topi[:, t, :], top[:, t, :], logit[:, t, :]))
            nc.vector.tensor_tensor(gw[:, :, 0:1], top[:, :, 1:2], top[:, :, 0:1], ALU.subtract).then_inc(topd_ready, 1)
            then_wait(nc.vector.tensor_copy(topf[:], topi[:]))
            for t in range(TT):
                for c in range(2):
                    then_wait(nc.vector.tensor_scalar(hot[:, t, c, :], eight[:], topf[:, t, c:c + 1], None, ALU.is_equal))
            then_wait(nc.vector.memset(pos[:], -1.0))
            then_wait(nc.vector.memset(gates[:], 0.0))
            nc.vector.tensor_tensor(hot[:, :, 2, :], hot[:, :, 0, :], hot[:, :, 1, :], ALU.add).then_inc(sel_ready, 1)
            dve.wait_ge(tope_ready, 1)
            then_wait(nc.vector.tensor_scalar(gw[:, :, 2:3], gw[:, :, 1:2], 1.0, None, ALU.add))
            then_wait(nc.vector.reciprocal(gw[:, :, 2:3], gw[:, :, 2:3]))
            then_wait(nc.vector.tensor_tensor(gw[:, :, 3:4], gw[:, :, 1:2], gw[:, :, 2:3], ALU.mult))
            for t in range(TT):
                then_wait(nc.vector.tensor_scalar(gates[:, t, 0:NE], hot[:, t, 0, :], gw[:, t, 2:3], None, ALU.mult))
                then_wait(nc.vector.scalar_tensor_tensor(gates[:, t, 0:NE], hot[:, t, 1, :], gw[:, t, 3:4], gates[:, t, 0:NE],
                                                         ALU.mult, ALU.add))
            then_wait(nc.vector.tensor_copy(gates[:, :, NE:2 * NE], gates[:, :, 0:NE]))
            dve.wait_ge(sel_ready, 1)
            dve.wait_ge(*full(l, "rank0"))
            nc.vector.scalar_tensor_tensor(pos[:, :, 0:NE], bank(l, "rank0")[:, 0:TT * NE].rearrange("p (t e) -> p t e", t=TT),
                                           1.0 / 8, hot[:, :, 2, :], ALU.mult, ALU.mult).then_inc(take(l, "rank0"), 1)
            dve.wait_ge(*taken(l, "rank0"))
            then_wait(nc.vector.tensor_scalar(pos[:, :, 0:NE], pos[:, :, 0:NE], -1.0, None, ALU.add))
            then_wait(nc.vector.tensor_scalar(pos[:, :, NE:2 * NE], pos[:, :, 0:NE], -float(PASS_CAP), None, ALU.add))
            dve.wait_ge(*full(l, "rank1"))
            nc.vector.tensor_reduce(cnt[0:1, 0:1], bank(l, "rank1")[0:1, 0:NE], AX_X, ALU.max).then_inc(take(l, "rank1"), 1)
            dve.wait_ge(*taken(l, "rank1"))
            nc.vector.tensor_scalar(npass[0:1, 0:1], cnt[0:1, 0:1], 8.0 * PASS_CAP, 1.0, ALU.is_gt, ALU.add
                                    ).then_inc(route_ready, 1)

            def hot_places(idx):
                for t in range(TT):
                    ins = nc.vector.tensor_scalar(oneh[:, t, :], place[:], pos[:, t, idx], None, ALU.is_equal)
                ins.then_inc(oneh_ready, 1)

            highs0 = HIGHS["passes"]
            PASS_HIGHS = FB + 2

            def gathered_low(count, bank_, take_):
                for i in range(2):
                    dve.wait_ge(acthigh_ready, count + i)
                    for k in range(4):
                        c = 4 * i + k
                        ins = act_low(xl[:, c, 0:PASS_CAP], bank_(f"ga{i}")[:, k * P:k * P + P], xh[:, c, 0:PASS_CAP],
                                      col(L - 1, "ffn", c))
                    ins.then_inc(take_(f"ga{i}"), 1)

            hot_places(slice(0, 1))
            dve.wait_ge(high_ready, NSPLIT + 1)
            dve.wait_ge(*pe_done_static(split_names[-2]))
            low(0, fill_width(0), 0)
            gathered_low(highs0 + 1, lambda n: bank(L - 1, n), lambda n: take(L - 1, n))

            dve.wait_ge(route_ready, 1)
            rounds = dve.value_load(npass[0:1, 0:1], min_val=1, max_val=2)
            with dve.Fori(0, rounds) as rnd:
                with dve.Fori(0, NE) as e:
                    p = rnd * NE + e
                    low_in_pass(1, p)
                    hot_places(bass.ds(p + 1, 1))
                    for t in range(TT):
                        ins = nc.vector.tensor_scalar(gated[:, t, :], place[:], pos[:, t, bass.ds(p, 1)], gates[:, t, bass.ds(p, 1)],
                                                      ALU.is_equal, ALU.mult)
                    ins.then_inc(gated_ready, 1)
                    for j in range(2, 2 * KT):
                        low_in_pass(j, p)
                    for i in range(FB):
                        a, b = i * BANK, min(i * BANK + BANK, DFF)
                        dve.wait_ge(*lfull(f"u{i}", p))
                        dve.wait_ge(*ltaken(f"g{i}", p))
                        nc.vector.tensor_tensor(h1[:, a:b], lbank(f"u{i}")[:, 0:b - a], h1[:, a:b], ALU.mult
                                                ).then_inc(ltake(f"u{i}"), 1)
                    low_in_pass(2 * KT, p)
                    dve.wait_ge(*lfull("GT", p))
                    nc.vector.tensor_copy(gatedT, lbank("GT")[:, 0:S]).then_inc(ltake("GT"), 1)
                    for i in range(FB):
                        k = min(4, FT - 4 * i)
                        dve.wait_ge(acthigh_ready, p * PASS_HIGHS + (highs0 + 2 + i + 1))
                        act_low(al[:, i * BANK:i * BANK + k * P], lbank(f"hT{i}")[:, 0:k * P],
                                ah[:, i * BANK:i * BANK + k * P]).then_inc(ltake(f"hT{i}"), 1)
                        if i == 1:
                            low_in_pass(2 * KT + 1, p)
                    low_in_pass(2 * KT + 2, p)
                    gathered_low(p * PASS_HIGHS + (highs0 + 2 + FB + 1), lbank, ltake)
                    for j in range(2 * KT + 3, PASS_FILLS):
                        low_in_pass(j, p)
                    low_in_pass(PASS_FILLS, p)
                    for t in range(TT):
                        for i in range(2):
                            dve.wait_ge(*lfull(f"sc{2 * t + i}", p))
                            xs = xres[:, t, i * BANK:i * BANK + BANK]
                            nc.vector.tensor_tensor(xs, xs, lbank(f"sc{2 * t + i}")[:], ALU.add
                                                    ).then_inc(ltake(f"sc{2 * t + i}"), 1)

        @block.tensor
        def _(pe):
            def open_bank(l, n):
                b, use = plan.at[l, n]
                if use > 0:
                    pe.wait_ge(psum_taken[b], use)
                return psum[b]

            def lopen(n, p):
                pe.wait_ge(psum_taken[in_pass.at[n][0]], lcount(n, p))
                return lbank(n)

            def done(l, n):
                return psum_full[plan.at[l, n][0]]

            def ldone(n):
                return psum_full[in_pass.at[n][0]]

            def weights(*name):
                n = fill_at[name]
                pe.wait_ge(slot_filled[n % NSLOT], 16 * (n // NSLOT + 1))
                k, c = fills[n][1]
                return ring[:, n % NSLOT, 0:k * c].rearrange("p (k c) -> p k c", k=k)

            def both(dst, x_high, x_low, w_high, first):
                nc.tensor.matmul(dst, x_high, w_high, start=first, stop=False)
                return nc.tensor.matmul(dst, x_low, w_high, start=False, stop=False)

            def mm(dst, lhsT, rhs, first, last):
                return nc.tensor.matmul(dst, lhsT, rhs, start=first, stop=last)

            def transposed(l, names, src):
                for i in range(4):
                    ps = open_bank(l, f"{names}{i}")
                    for k in range(2):
                        for t in range(TT):
                            c = (2 * i + k) * P
                            ins = nc.tensor.transpose(ps[:, k * S + t * P:k * S + t * P + P], src[:, t, c:c + P], ident[:])
                    ins.then_inc(done(l, f"{names}{i}"), 1)

            def channel_tile(ps, fill, width, c, ends, last_end, inputs=None):
                n = split_at[fill]
                pe.wait_ge(low_ready, n + 1)
                w_high = wh[:, n % 2, 0:KT * width].rearrange("p (k c) -> p k c", k=KT)[:, :, c:c + P]
                w_low = wl[:, n % 2, 0:KT * width].rearrange("p (k c) -> p k c", k=KT)[:, :, c:c + P]
                for k in range(KT):
                    if inputs is not None and k % 2 == 0:
                        pe.wait_ge(*taken(fill[0], f"{inputs}{k // 2}"))
                    mm(ps, w_high[:, k, :], aT[:, k, :], k == 0, False)
                    ins = mm(ps, w_high[:, k, :], aT_low[:, k, :], False, False)
                if ends:
                    ins.then_inc(highs_used, 1)
                for k in range(KT):
                    ins = mm(ps, w_low[:, k, :], aT[:, k, :], False, k == KT - 1)
                if last_end is not None:
                    ins.then_inc(last_end, 1)
                elif ends:
                    ins.then_inc(slots_used, 1)

            def token_tile(ps, fill, width, a, b, t, ends, last_end):
                n, ts = split_at[fill], slice(t * P, t * P + P)
                pe.wait_ge(low_ready, n + 1)
                w_high = wh[:, n % 2, 0:KT * width].rearrange("p (k c) -> p k c", k=KT)[:, :, a:b]
                w_low = wl[:, n % 2, 0:KT * width].rearrange("p (k c) -> p k c", k=KT)[:, :, a:b]
                for k in range(KT):
                    ins = both(ps, aT[:, k, ts], aT_low[:, k, ts], w_high[:, k, :], k == 0)
                if ends:
                    ins.then_inc(highs_used, 1)
                for k in range(KT):
                    ins = mm(ps, aT[:, k, ts], w_low[:, k, :], False, k == KT - 1)
                if last_end is not None:
                    ins.then_inc(last_end, 1)
                elif ends:
                    ins.then_inc(slots_used, 1)

            def logits(l, n, names, bias, product):
                ps = open_bank(l, n)
                for t in range(TT):
                    for k in range(KT):
                        if t == 0 and k % 2 == 0:
                            pe.wait_ge(*taken(l, f"{names}{k // 2}"))
                        product(ps[:, 8 * t:8 * t + 8], k, slice(t * P, t * P + P))
                    ins = mm(ps[:, 8 * t:8 * t + 8], ones1[:], bias, False, True)
                ins.then_inc(done(l, n), 1)

            def forget_product(l):
                def product(ps, k, ts):
                    both(ps, aT[:, k, ts], aT_low[:, k, ts], wf_high[:, KT * l + k, :], k == 0)
                    mm(ps, aT[:, k, ts], wf_low[:, KT * l + k, :], False, False)
                return product

            def router_product(ps, k, ts):
                mm(ps, hT[:, k, ts], wr[:, k, :], k == 0, False)

            def mean_rows(l, n, sel, at, width, src, tiles):
                ps = open_bank(l, n)
                for j in range(tiles):
                    step = at - (2 * j if width != 4 else j)
                    ins = mm(ps[0:width, 0:S], sel[:, step:step + width], src[:, j, :], j == 0, j == tiles - 1)
                ins.then_inc(done(l, n), 1)

            def spread_rows(l, names, spread, rows, tiles):
                for i in range(tiles // 2):
                    ps = open_bank(l, f"{names}{i}")
                    for k in range(2):
                        c = (2 * i + k) * P
                        ins = mm(ps[:, k * S:k * S + S], spread[:, c:c + P], rows, True, True)
                    ins.then_inc(done(l, f"{names}{i}"), 1)

            def gather(open_, done_):
                for i in range(2):
                    ps = open_(f"ga{i}")
                    for k in range(4):
                        c = (4 * i + k) * P
                        for t in range(TT):
                            ins = mm(ps[:, k * P:k * P + P], xn[:, t, c:c + P], oneh[:, t, :], t == 0, t == TT - 1)
                    ins.then_inc(done_(f"ga{i}"), 1)

            def bank_cols(i):
                return i * BANK, min(i * BANK + BANK, DFF)

            pe.wait_ge(ident_ready, 1)
            pe.wait_ge(params_loaded, 16 * NPARAMS)
            ps = open_bank(0, "vec")
            nc.tensor.transpose(ps[:, 0:2 * NV], vrows, ident[0:2 * NV, 0:2 * NV]).then_inc(done(0, "vec"), 1)
            for l in range(L):
                pe.wait_ge(xn_ready, XN[l, "mix"])
                transposed(l, "xT", xn)
                if l == 0:
                    pe.wait_ge(consts_ready, 1)
                    pe.wait_ge(wf_split, 2)
                logits(l, "f", "xT", brow[0:1, l * FH:l * FH + FH], forget_product(l))
                if l == 0:
                    pe.wait_ge(xn_ready, XN[0, "mem"])
                    transposed(0, "mT", memraw)
                for i in range(4):
                    ps = open_bank(l, f"qk{i}")
                    for c in (2 * i, 2 * i + 1):
                        channel_tile(ps[:, (c % 2) * S:(c % 2) * S + S], (l, "z", c // 3), ZCOLS, (c % 3) * P, c % 3 == 2,
                                     done(l, f"qk{i}") if c % 2 else None)
                for t in range(TT):
                    token_tile(open_bank(l, f"v{t}")[:, 0:P], (l, "z", 2), ZCOLS, 2 * P, 3 * P, t, t == TT - 1, None)
                for t in range(TT):
                    token_tile(bank(l, f"v{t}")[:, P:4 * P], (l, "z", 3), ZCOLS, 0, 3 * P, t, t == TT - 1, done(l, f"v{t}"))
                pe.wait_ge(squares_ready, SQUARES[l, "qk3"])
                mean_rows(l, "ssqk", selg, 14, 16, sq, 8)
                for i in range(6):
                    ps = open_bank(l, f"conv{i}")
                    for c in (2 * i, 2 * i + 1):
                        channel_tile(ps[:, (c % 2) * S:(c % 2) * S + S], (l, "z", 4 + c // 3), ZCOLS, (c % 3) * P, c % 3 == 2,
                                     done(l, f"conv{i}") if c % 2 else None)
                pe.wait_ge(rows_ready, ROWS[l, "qk"])
                spread_rows(l, "bq", spreadg[:], mqk[:], 8)
                pe.wait_ge(decay_ready, l + 1)
                for i in range(4):
                    pe.wait_ge(*taken(l, f"bq{i}"))
                for h in range(FH):
                    r, j = (h % 2) * HD, h // 2
                    q, k = zqk[r:r + HD, j, :], zqk[r:r + HD, 4 + j, :]
                    ps = open_bank(l, f"s{h}")
                    mm(ps[:, 0:P], q[:, 0:P], k[:, 0:P], True, False)
                    mm(ps[:, 0:P], decay[:, h, 0:P], after[:, 0:P], False, True)
                    mm(ps[:, P:3 * P], q[:, P:S], k, True, False)
                    mm(ps[:, P:2 * P], decay[:, h, P:S], after[:, 0:P], False, False)
                    mm(ps[:, P:3 * P], decay[:, h, S:3 * P], after[:, P:3 * P], False, True).then_inc(done(l, f"s{h}"), 1)
                pe.wait_ge(memg_ready, l + 1)
                for i in range(2):
                    ps = open_bank(l, f"mk{i}")
                    for c in range(2):
                        channel_tile(ps[:, c * S:c * S + S], (l, "xkv", i), 256, c * P, c == 1, done(l, f"mk{i}") if c else None)
                for s in range(2):
                    for t in range(TT):
                        ps = open_bank(l, f"mv{t}") if s == 0 else bank(l, f"mv{t}")
                        token_tile(ps[:, 256 * s:256 * s + 256], (l, "xkv", 2 + s), 256, 0, 256, t, t == TT - 1,
                                   done(l, f"mv{t}") if s else None)
                pe.wait_ge(squares_ready, SQUARES[l, "cv"])
                mean_rows(l, "ssc", selg, 14, 8, zc[:, 4:8, :], 4)
                mean_rows(l, "ssmk", selh, 3, 4, ksq, XH)
                def probs_transposed(heads):
                    for h in heads:
                        pe.wait_ge(probs_ready, 2 * FH * l + 2 * h + 2)
                        ps = open_bank(l, f"pt{h}")
                        for c in range(3):
                            ins = nc.tensor.transpose(ps[:, c * P:c * P + P], sc[:, h, c * P:c * P + P], ident[:])
                        ins.then_inc(done(l, f"pt{h}"), 1)

                probs_transposed(range(4))
                pe.wait_ge(rows_ready, ROWS[l, "cv"])
                spread_rows(l, "bc", spreadg[0:8, :], mcv[:], 4)
                pe.wait_ge(rows_ready, ROWS[l, "mk"])
                spread_rows(l, "bmk", spreadh[:], mmk[:], XH)
                probs_transposed(range(4, FH))
                for t in range(TT):
                    pe.wait_ge(*taken(l, f"v{t}"))
                for q in range(2):
                    ps = open_bank(l, f"o{q}")
                    for h in range(FH):
                        if q == 0:
                            pe.wait_ge(*taken(l, f"pt{h}"))
                        for t in range(q + 1):
                            c = (q + t) * P
                            ins = mm(ps[:, h * HD:h * HD + HD], pT[:, h, c:c + P], vtok[:, t, h * HD:h * HD + HD], t == 0, t == q)
                    ins.then_inc(done(l, f"o{q}"), 1)
                def token_projection(names, fill, rows, ks, src, waits):
                    for k in ks:
                        w = weights(l, fill, k // 2)
                        for n in waits.get(k, ()):
                            pe.wait_ge(*taken(l, n))
                        for i in range(4):
                            t, half = i // 2, i % 2
                            ps = open_bank(l, f"{names}{i}") if k == 0 else bank(l, f"{names}{i}")
                            ins = mm(ps[:], src[:, k, t * P:t * P + P], w[:, k % 2, half * BANK:half * BANK + BANK],
                                     k == 0, k == rows - 1)
                            if k == rows - 1:
                                ins.then_inc(done(l, f"{names}{i}"), 1)
                        if k < rows - 1 and k % 2 == 1:
                            ins.then_inc(slots_used, 1)

                token_projection("wo", "wo", KT, range(4), yT, {0: ("bc0", "bc1")})
                pe.wait_ge(onorm_ready, l + 1)
                for i in range(2):
                    ps = open_bank(l, f"oT{i}")
                    for k in range(2):
                        for t in range(TT):
                            c = (2 * i + k) * P
                            ins = nc.tensor.transpose(ps[:, k * S + t * P:k * S + t * P + P], otok[:, t, c:c + P], ident[:])
                    ins.then_inc(done(l, f"oT{i}"), 1)
                token_projection("wo", "wo", KT, range(4, KT), yT, {4: ("oT0",), 6: ("oT1",)})

                pe.wait_ge(xn_ready, XN[l, "xa"])
                transposed(l, "yT", xn)
                for i in range(2):
                    ps = open_bank(l, f"xq{i}")
                    for c in range(2):
                        channel_tile(ps[:, c * S:c * S + S], (l, "xq", i), 256, c * P, c == 1, done(l, f"xq{i}") if c else None,
                                     "yT" if i + c == 0 else None)
                pe.wait_ge(squares_ready, SQUARES[l, "xq"])
                mean_rows(l, "ssxq", selh, 3, 4, sq, XH)
                pe.wait_ge(rows_ready, ROWS[l, "xq"])
                spread_rows(l, "bxq", spreadh[:], mxq[:], XH)
                for i in range(2):
                    pe.wait_ge(*taken(l, f"bmk{i}"))
                for h in range(XH):
                    ps = open_bank(l, f"xs{h}")
                    pe.wait_ge(*taken(l, f"bxq{h // 2}"))
                    for q in range(2):
                        ins = mm(ps[:, q * S:q * S + S], zqk[:, h, q * P:q * P + P], xk[:, h, :], True, True)
                    ins.then_inc(done(l, f"xs{h}"), 1)
                for h in range(XH):
                    ps = open_bank(l, f"xpt{h}")
                    pe.wait_ge(xpn_ready, XH * l + h + 1)
                    for m in range(2):
                        for q in range(2):
                            ins = nc.tensor.transpose(ps[:, m * S + q * P:m * S + q * P + P], xsc[:, h, q, m * P:m * P + P], ident[:])
                    ins.then_inc(done(l, f"xpt{h}"), 1)
                for t in range(TT):
                    pe.wait_ge(*taken(l, f"mv{t}"))
                for i in range(2):
                    ps = open_bank(l, f"xo{i}")
                    for h in (2 * i, 2 * i + 1):
                        pe.wait_ge(*taken(l, f"xpt{h}"))
                        for m in range(2):
                            ins = mm(ps[:, (h % 2) * S:(h % 2) * S + S], xv[:, m, h * XHD:h * XHD + XHD], xpT[:, h, m, :], m == 0, m == 1)
                    ins.then_inc(done(l, f"xo{i}"), 1)
                token_projection("xw", "xo", XH, range(XH), zqk[:, 4:8, :], {0: ("xo0",), 2: ("xo1",)})

                pe.wait_ge(xn_ready, XN[l, "ffn"])
                transposed(l, "zT", xn)
                if l == 0:
                    for half in range(2):
                        base = split_at[0, "g", half, 0]
                        for m, part_ in enumerate(("g", "u")):
                            for s in range(KT // 2):
                                n = base + m * (KT // 2) + s
                                products = [(k, t, i, (k % 2) * HALF + i * BANK, min(BANK, HALF - i * BANK))
                                            for k in (2 * s, 2 * s + 1) for t in range(TT) for i in range(HB)]
                                if half == 0 and m == 0:
                                    pe.wait_ge(*taken(0, f"zT{s}"))
                                pe.wait_ge(high_ready, n + 1)
                                for k, t, i, c, width in products:
                                    r, ts = f"{part_}{half}{t}{i}", slice(t * P, t * P + P)
                                    if (k, t, i) == (2 * s + 1, TT - 1, HB - 1):
                                        pe.wait_ge(low_ready, n + 1)
                                    ps = open_bank(0, r) if k == 0 else bank(0, r)
                                    ins = both(ps[:, 0:width], xh[:, k, ts], xl[:, k, ts], wh[:, n % 2, c:c + width], k == 0)
                                ins.then_inc(highs_used, 1)
                                for k, t, i, c, width in products:
                                    r, ts = f"{part_}{half}{t}{i}", slice(t * P, t * P + P)
                                    ins = mm(bank(0, r)[:, 0:width], xh[:, k, ts], wl[:, n % 2, c:c + width], False, k == KT - 1)
                                    if k == KT - 1:
                                        ins.then_inc(done(0, r), 1)
                                if s < KT // 2 - 1:
                                    ins.then_inc(slots_used, 1)
                        for t in range(TT):
                            for i in range(HB):
                                pe.wait_ge(*taken(0, f"u{half}{t}{i}"))
                        for i in range(-(-HT // 2)):
                            ps = open_bank(0, f"hT{half}{i}")
                            for j in range(2 * i, min(2 * i + 2, HT)):
                                for t in range(TT):
                                    c = (j % 2) * S + t * P
                                    ins = nc.tensor.transpose(ps[:, c:c + P], hid[:, t, j * P:j * P + P], ident[:])
                            ins.then_inc(done(0, f"hT{half}{i}"), 1)
                        banks = [open_bank(0, f"d{half}{i // 2}{i % 2}") for i in range(4)]
                        for s in range(HSLOT):
                            n = base + KT + s
                            last = min(DROWS * s + DROWS, HT) - 1
                            products = [(j, q, j * S + (q // 2) * P, (j % DROWS) * D + (q % 2) * BANK)
                                        for j in range(DROWS * s, last + 1) for q in range(4)]
                            pe.wait_ge(high_ready, n + 1)
                            for j, q, a, c in products:
                                if q == 0 and j % 2 == 0:
                                    pe.wait_ge(*taken(0, f"hT{half}{j // 2}"))
                                if (j, q) == (last, 3):
                                    pe.wait_ge(low_ready, n + 1)
                                ins = both(banks[q][:], ah[:, a:a + P], al[:, a:a + P], wh[:, n % 2, c:c + BANK], j == 0)
                            ins.then_inc(highs_used, 1)
                            for j, q, a, c in products:
                                ins = mm(banks[q][:], ah[:, a:a + P], wl[:, n % 2, c:c + BANK], False, j == HT - 1)
                                if j == HT - 1:
                                    ins.then_inc(done(0, f"d{half}{q // 2}{q % 2}"), 1)
                            if last < HT - 1:
                                ins.then_inc(slots_used, 1)

            l = L - 1
            logits(l, "r", "zT", brow[0:1, L * FH:L * FH + NE], router_product)
            pe.wait_ge(sel_ready, 1)
            ps = open_bank(l, "rank0")
            mm(ps[:, 0:NE], tri8[:, 0:P], hot[:, 0, 2, :], True, True)
            mm(ps[:, NE:2 * NE], tri8[:, P:S], hot[:, 0, 2, :], True, False)
            mm(ps[:, NE:2 * NE], tri8[:, 0:P], hot[:, 1, 2, :], False, True).then_inc(done(l, "rank0"), 1)
            ps = open_bank(l, "rank1")
            mm(ps[0:1, 0:NE], tri8[:, P:P + 1], hot[:, 0, 2, :], True, False)
            mm(ps[0:1, 0:NE], tri8[:, P:P + 1], hot[:, 1, 2, :], False, True).then_inc(done(l, "rank1"), 1)
            pe.wait_ge(oneh_ready, 1)
            gather(lambda n: open_bank(l, n), lambda n: done(l, n))
            for i in range(2):
                pe.wait_ge(*taken(l, f"ga{i}"))

            pe.wait_ge(route_ready, 1)
            rounds = pe.value_load(npass[0:1, 0:1], min_val=1, max_val=2)
            with pe.Fori(0, rounds) as rnd:
                with pe.Fori(0, NE) as e:
                    p = rnd * NE + e
                    for half, names in enumerate(("g", "u")):
                        for k in range(KT):
                            j = half * KT + k
                            pe.wait_ge(high_ready, p * PASS_FILLS + (NSPLIT + j + 1))
                            for i in range(FB):
                                a, b = bank_cols(i)
                                if i == FB - 1:
                                    pe.wait_ge(low_ready, p * PASS_FILLS + (NSPLIT + j + 1))
                                ps = lopen(f"{names}{i}", p) if k == 0 else lbank(f"{names}{i}")
                                ins = both(ps[:, 0:b - a], xh[:, k, 0:PASS_CAP], xl[:, k, 0:PASS_CAP], wh[:, j % 2, a:b], k == 0)
                            ins.then_inc(highs_used, 1)
                            for i in range(FB):
                                a, b = bank_cols(i)
                                ins = mm(lbank(f"{names}{i}")[:, 0:b - a], xh[:, k, 0:PASS_CAP], wl[:, j % 2, a:b], False, k == KT - 1)
                                if k == KT - 1:
                                    ins.then_inc(ldone(f"{names}{i}"), 1)
                            if k < KT - 1:
                                ins.then_inc(slots_used, 1)
                    pe.wait_ge(gated_ready, p + 1)
                    ps = lopen("GT", p)
                    for t in range(TT):
                        ins = nc.tensor.transpose(ps[:, t * P:t * P + P], gated[:, t, :], ident[:])
                    ins.then_inc(ldone("GT"), 1)
                    for i in range(FB):
                        pe.wait_ge(*ltaken(f"u{i}", p))
                        ps = lopen(f"hT{i}", p)
                        for j in range(4 * i, min(4 * i + 4, FT)):
                            ins = nc.tensor.transpose(ps[:, (j % 4) * P:(j % 4) * P + P], h1[:, j * P:j * P + P], ident[:])
                        ins.then_inc(ldone(f"hT{i}"), 1)
                    pe.wait_ge(oneh_ready, p + 2)
                    gather(lambda n: lopen(n, p), ldone)
                    banks = [lopen(f"d{i}", p) for i in range(2)]
                    for s in range(DSLOT):
                        n = 2 * KT + s
                        last = min(DROWS * s + DROWS, FT) - 1
                        products = [(j, i, (j % DROWS) * D + i * BANK) for j in range(DROWS * s, last + 1) for i in range(2)]
                        pe.wait_ge(high_ready, p * PASS_FILLS + (NSPLIT + n + 1))
                        for j, i, c in products:
                            if i == 0 and j % 4 == 0:
                                pe.wait_ge(*ltaken(f"hT{j // 4}", p))
                            if (j, i) == (last, 1):
                                pe.wait_ge(low_ready, p * PASS_FILLS + (NSPLIT + n + 1))
                            ins = both(banks[i][:], ah[:, j * P:j * P + P], al[:, j * P:j * P + P], wh[:, n % 2, c:c + BANK], j == 0)
                        ins.then_inc(highs_used, 1)
                        for j, i, c in products:
                            ins = mm(banks[i][:], ah[:, j * P:j * P + P], wl[:, n % 2, c:c + BANK], False, j == FT - 1)
                            if j == FT - 1:
                                ins.then_inc(ldone(f"d{i}"), 1)
                        if last < FT - 1:
                            ins.then_inc(slots_used, 1)
                    pe.wait_ge(*ltaken("GT", p))
                    for t in range(TT):
                        for i in range(2):
                            ps = lopen(f"sc{2 * t + i}", p)
                            pe.wait_ge(*ltaken(f"d{i}", p))
                            mm(ps[:], gatedT[:, t * P:t * P + P], yexp[:, i * BANK:i * BANK + BANK], True, True
                               ).then_inc(ldone(f"sc{2 * t + i}"), 1)
                    for i in range(2):
                        pe.wait_ge(*ltaken(f"ga{i}", p))


_INS = ['x', 'mem', 'g_mix', 'w_in', 'conv_w', 'b_f', 'g_q', 'g_k', 'g_conv_out', 'g_fox_out', 'w_out',
        'g_xa', 'g_mem', 'w_xq', 'w_xkv', 'g_xq', 'g_xk', 'w_xo', 'g_ffn', 'w_gate', 'w_up', 'w_down',
        'w_router', 'b_router', 'we_gate', 'we_up', 'we_down']


def kernel(**inputs):
    import concourse.bacc as bacc
    from concourse.bass_utils import run_bass_kernel_spmd

    nc = bacc.Bacc("TRN2", target_bir_lowering=False, num_devices=1)
    arrays, args = {}, []
    for name in _INS:
        a = np.ascontiguousarray(inputs[name])
        arrays[f"in_{name}"] = a
        args.append(nc.dram_tensor(f"in_{name}", a.shape, mybir.dt.from_np(a.dtype), kind="ExternalInput").ap())
    out = nc.dram_tensor("out_x", arrays["in_x"].shape, F32, kind="ExternalOutput").ap()
    build(nc, *args, out)
    r = run_bass_kernel_spmd(nc, [arrays], core_ids=[0])
    return r.results[0]["out_x"]
```
